# Optimizing a Trainium2 kernel written in Bass

```python
import jax
import jax.numpy as jnp
from jax import lax

D_MODEL = 2048
BATCH = 1
SEQ = 256
DEPTH = 1

CHUNK = 64
Q_BLOCK = 128
EPS = 1e-6

DN_QK_HEADS = 16
DN_V_HEADS = 32
DN_HEAD_DIM = 128
DN_QK_DIM = DN_QK_HEADS * DN_HEAD_DIM
DN_V_DIM = DN_V_HEADS * DN_HEAD_DIM
DN_CONV_DIM = 2 * DN_QK_DIM + DN_V_DIM
CONV_K = 4

FOX_HEADS = 16
FOX_HEAD_DIM = 128
FOX_DIM = FOX_HEADS * FOX_HEAD_DIM

N_BRANCH = 2
FFN_HIDDEN = -(-8 * D_MODEL // (3 * 256)) * 256

IN_SIZES = (DN_CONV_DIM, DN_V_DIM, DN_V_HEADS, DN_V_HEADS, 3 * FOX_DIM, FOX_HEADS, N_BRANCH * D_MODEL)
N_IN = sum(IN_SIZES)
IN_OFFSETS = tuple(sum(IN_SIZES[:i + 1]) for i in range(len(IN_SIZES) - 1))

kernel_name = 'hybrid_deltanet_fox_adaln_block'

def rmsnorm(x, gain):
    xf = x.astype(jnp.float32)
    y = xf * lax.rsqrt(jnp.mean(xf * xf, axis=-1, keepdims=True) + EPS)
    return (y * gain.astype(jnp.float32)).astype(x.dtype)

def l2norm(x):
    return x * lax.rsqrt(jnp.sum(x * x, axis=-1, keepdims=True) + EPS)

def causal_short_conv(u, w):
    t = u.shape[1]
    up = jnp.pad(u, ((0, 0), (CONV_K - 1, 0), (0, 0)))
    out = up[:, 0:t, :] * w[:, 0]
    for j in range(1, CONV_K):
        out = out + up[:, j:j + t, :] * w[:, j]
    return out

def chunk_gated_delta_rule(q, k, v, g, beta):
    b, t, h, dk = q.shape
    dv = v.shape[-1]
    n = t // CHUNK
    f32 = jnp.float32
    q = l2norm(q.astype(f32)) * dk ** -0.5
    k = l2norm(k.astype(f32))
    v = v.astype(f32)

    def blocks(a):
        return a.reshape(b, n, CHUNK, h, -1).transpose(0, 3, 1, 2, 4)

    q, k, v = blocks(q), blocks(k), blocks(v)
    beta = beta.astype(f32).reshape(b, n, CHUNK, h).transpose(0, 3, 1, 2)
    gc = jnp.cumsum(g.astype(f32).reshape(b, n, CHUNK, h).transpose(0, 3, 1, 2), axis=-1)
    causal = jnp.tril(jnp.ones((CHUNK, CHUNK), dtype=bool))
    strict = jnp.tril(jnp.ones((CHUNK, CHUNK), dtype=bool), -1)
    decay = jnp.exp(jnp.where(causal, gc[..., :, None] - gc[..., None, :], -jnp.inf))
    k_beta = k * beta[..., None]
    v_beta = v * beta[..., None]
    lower = jnp.where(strict, jnp.einsum('bhncd,bhnsd->bhncs', k_beta, k) * decay, 0.0)
    a_mat = lower + jnp.eye(CHUNK, dtype=f32)
    u = lax.linalg.triangular_solve(a_mat, v_beta, left_side=True, lower=True, unit_diagonal=True)
    w = lax.linalg.triangular_solve(a_mat, k_beta * jnp.exp(gc)[..., None], left_side=True, lower=True,
                                    unit_diagonal=True)
    attn = jnp.einsum('bhncd,bhnsd->bhncs', q, k) * decay

    def step(state, xs):
        q_i, k_i, u_i, w_i, attn_i, gc_i = xs
        v_new = u_i - jnp.einsum('bhcd,bhde->bhce', w_i, state)
        o = (jnp.einsum('bhcd,bhde->bhce', q_i * jnp.exp(gc_i)[..., None], state)
             + jnp.einsum('bhcs,bhse->bhce', attn_i, v_new))
        g_last = gc_i[..., -1]
        state = (state * jnp.exp(g_last)[..., None, None]
                 + jnp.einsum('bhcd,bhce->bhde', k_i * jnp.exp(g_last[..., None] - gc_i)[..., None], v_new))
        return state, o

    xs = tuple(jnp.moveaxis(a, 2, 0) for a in (q, k, u, w, attn, gc))
    _, o = lax.scan(step, jnp.zeros((b, h, dk, dv), f32), xs)
    return o.transpose(1, 0, 3, 2, 4).reshape(b, t, h, dv)

def forgetting_attention(q, k, v, log_f):
    b, t, h, d = q.shape
    f32 = jnp.float32
    q, k, v = q.astype(f32), k.astype(f32), v.astype(f32)
    cum_f = jnp.cumsum(log_f.astype(f32), axis=1)
    nb = t // Q_BLOCK
    qb = q.reshape(b, nb, Q_BLOCK, h, d).transpose(1, 0, 3, 2, 4)
    fq = cum_f.reshape(b, nb, Q_BLOCK, h).transpose(1, 0, 3, 2)
    fk = cum_f.transpose(0, 2, 1)
    pos_k = jnp.arange(t)
    scale = d ** -0.5

    def block(args):
        i, q_i, f_i = args
        s = jnp.einsum('bhqd,bkhd->bhqk', q_i, k) * scale + f_i[..., None] - fk[:, :, None, :]
        pos_q = i * Q_BLOCK + jnp.arange(Q_BLOCK)
        s = jnp.where(pos_k[None, :] <= pos_q[:, None], s, -jnp.inf)
        p = jax.nn.softmax(s, axis=-1)
        return jnp.einsum('bhqk,bkhd->bqhd', p, v)

    o = lax.map(block, (jnp.arange(nb), qb, fq))
    return o.transpose(1, 0, 2, 3, 4).reshape(b, t, h, d)

def hybrid_mixer(h, w_in, conv_w, a_log, dt_bias, norm_w, f_bias, w_br_dn, w_br_fox, w_out):
    b, t, _ = h.shape
    f32 = jnp.float32
    proj = h @ w_in
    dn_qkv, dn_z, dn_b, dn_a, fox_qkv, fox_f, merge = jnp.split(proj, IN_OFFSETS, axis=-1)

    dn_qkv = jax.nn.silu(causal_short_conv(dn_qkv, conv_w))
    q, k, v = jnp.split(dn_qkv, (DN_QK_DIM, 2 * DN_QK_DIM), axis=-1)
    rep = DN_V_HEADS // DN_QK_HEADS
    q = jnp.repeat(q.reshape(b, t, DN_QK_HEADS, DN_HEAD_DIM), rep, axis=2)
    k = jnp.repeat(k.reshape(b, t, DN_QK_HEADS, DN_HEAD_DIM), rep, axis=2)
    v = v.reshape(b, t, DN_V_HEADS, DN_HEAD_DIM)
    beta = jax.nn.sigmoid(dn_b.astype(f32))
    g = -jnp.exp(a_log.astype(f32)) * jax.nn.softplus(dn_a.astype(f32) + dt_bias.astype(f32))
    o_dn = chunk_gated_delta_rule(q, k, v, g, beta)
    z = dn_z.reshape(b, t, DN_V_HEADS, DN_HEAD_DIM).astype(f32)
    o_dn = rmsnorm(o_dn, norm_w) * jax.nn.silu(z)
    y_dn = o_dn.reshape(b, t, DN_V_DIM).astype(h.dtype) @ w_br_dn

    fq, fk, fv = jnp.split(fox_qkv, 3, axis=-1)
    shp = (b, t, FOX_HEADS, FOX_HEAD_DIM)
    log_f = jax.nn.log_sigmoid(fox_f.astype(f32) + f_bias.astype(f32))
    o_fox = forgetting_attention(fq.reshape(shp), fk.reshape(shp), fv.reshape(shp), log_f)
    y_fox = o_fox.reshape(b, t, FOX_DIM).astype(h.dtype) @ w_br_fox

    gate_dn, gate_fox = jnp.split(jax.nn.sigmoid(merge), N_BRANCH, axis=-1)
    return (gate_dn * y_dn + gate_fox * y_fox) @ w_out

def swiglu(h, w_gate, w_up, w_down):
    return (jax.nn.silu(h @ w_gate) * (h @ w_up)) @ w_down

def setup_inputs(seed: int = 0) -> dict:
    key = jax.random.key(seed)
    ks = jax.random.split(key, 20)
    L, D, F = DEPTH, D_MODEL, FFN_HIDDEN
    f32 = jnp.float32

    def nrm(k, shape, fan_in):
        return jax.random.normal(k, shape, f32) * fan_in ** -0.5

    x = jax.random.normal(ks[0], (BATCH, SEQ, D), f32)
    c = jax.random.normal(ks[1], (BATCH, D), f32)
    w_ada = nrm(ks[2], (L, D, 6 * D), D)
    b_ada = 0.02 * jax.random.normal(ks[3], (L, 6 * D), f32)
    norm_gains = 1.0 + 0.05 * jax.random.normal(ks[4], (L, 4, D), f32)
    w_in = nrm(ks[5], (L, D, N_IN), D)
    dn_conv = nrm(ks[6], (L, DN_CONV_DIM, CONV_K), CONV_K)
    dn_a_log = jnp.log(jax.random.uniform(ks[7], (L, DN_V_HEADS), f32, 1.0, 16.0))
    dt = jnp.exp(jax.random.uniform(ks[8], (L, DN_V_HEADS), f32, jnp.log(1e-3), jnp.log(1e-1)))
    dn_dt_bias = dt + jnp.log(-jnp.expm1(-dt))
    dn_norm_w = 1.0 + 0.05 * jax.random.normal(ks[9], (L, DN_HEAD_DIM), f32)
    fox_f_bias = jax.random.uniform(ks[10], (L, FOX_HEADS), f32, 1.0, 4.0)
    w_branch_dn = nrm(ks[11], (L, DN_V_DIM, D), DN_V_DIM)
    w_branch_fox = nrm(ks[12], (L, FOX_DIM, D), FOX_DIM)
    w_out = nrm(ks[13], (L, D, D), D)
    w_gate = nrm(ks[14], (L, D, F), D)
    w_up = nrm(ks[15], (L, D, F), D)
    w_down = nrm(ks[16], (L, F, D), F)
    return {'x': x, 'c': c, 'w_ada': w_ada, 'b_ada': b_ada, 'norm_gains': norm_gains, 'w_in': w_in,
            'dn_conv': dn_conv, 'dn_a_log': dn_a_log, 'dn_dt_bias': dn_dt_bias, 'dn_norm_w': dn_norm_w,
            'fox_f_bias': fox_f_bias, 'w_branch_dn': w_branch_dn, 'w_branch_fox': w_branch_fox,
            'w_out': w_out, 'w_gate': w_gate, 'w_up': w_up, 'w_down': w_down}

def reference(x, c, w_ada, b_ada, norm_gains, w_in, dn_conv, dn_a_log, dn_dt_bias, dn_norm_w,
              fox_f_bias, w_branch_dn, w_branch_fox, w_out, w_gate, w_up, w_down):
    cond = jax.nn.silu(c)
    for l in range(DEPTH):
        mod = (cond @ w_ada[l] + b_ada[l])[:, None, :]
        shift_m, scale_m, gate_m, shift_f, scale_f, gate_f = jnp.split(mod, 6, axis=-1)
        h = rmsnorm(x, norm_gains[l, 0]) * (1.0 + scale_m) + shift_m
        y = hybrid_mixer(h, w_in[l], dn_conv[l], dn_a_log[l], dn_dt_bias[l], dn_norm_w[l],
                         fox_f_bias[l], w_branch_dn[l], w_branch_fox[l], w_out[l])
        x = x + gate_m * rmsnorm(y, norm_gains[l, 1])
        h = rmsnorm(x, norm_gains[l, 2]) * (1.0 + scale_f) + shift_f
        y = swiglu(h, w_gate[l], w_up[l], w_down[l])
        x = x + gate_f * rmsnorm(y, norm_gains[l, 3])
    return x


_drawn_inputs = setup_inputs


def setup_inputs(seed=0):
    import zlib

    import numpy as np

    out = dict(_drawn_inputs(seed))
    spreads = {}
    factors = {}
    for name, (base, spread) in spreads.items():
        noise = np.random.default_rng([zlib.crc32(name.encode()), seed]).standard_normal(out[name].shape)
        drawn = base * np.exp(spread * noise) if base else spread * noise
        out[name] = jnp.asarray(drawn.astype(out[name].dtype))
    for name, factor in factors.items():
        out[name] = (out[name] * factor).astype(out[name].dtype)
    return out
```

```python
from contextlib import ExitStack

import concourse.bass as bass
from concourse import mybir

F32 = mybir.dt.float32
F32R = mybir.dt.float32r
ALU = mybir.AluOpType
ACT = mybir.ActivationFunctionType
AX = mybir.AxisListType

P = 128
D = 2048
T = 256
KD = D // P
TT = T // P
QKH, VH, FH = 16, 32, 16
CONV_K = 4
QK_DIM, V_DIM = QKH * P, VH * P
CONV_DIM = 2 * QK_DIM + V_DIM
FOX = FH * P
FFN = 5632
KF = FFN // P
EPS = 1e-6
OFF_Z = CONV_DIM
OFF_B = OFF_Z + V_DIM
OFF_FOX = OFF_B + 2 * VH
OFF_F = OFF_FOX + 3 * FOX
OFF_M = OFF_F + FH
SMALL = 2 * VH + FH
GATES = VH + FH
TILE = 2048
GROUP = 512
RAW, SPLIT, ADA = 4, 2, 4
HALVES = ((0, 2), (2, 4))
ADA_COLS = 4 * D // QKH
ADA_PIECES = 8

SLOTS = 24
QUARTERS = (2, 2, 1, 1, 2, 2, 0) + (1, 0) * 5 + (2, 1, 1, 1, 1, 1, 2)
RUNS = [range(sum(QUARTERS[:s]), sum(QUARTERS[:s + 1])) for s in range(SLOTS)]
END = [next(s for s in range(SLOTS) if 4 * b + 3 in RUNS[s]) for b in range(6)]
ADA_SLOTS = range(6, 22)
CONV_SLOTS = (2, 7, 11, 18)
TRANSPOSED = 5
LEVELS = 7
SCALE = float(P) ** -0.5
SQD = float(P) ** 0.5
MASKED = -1e30
FREE = 2

HEADS_A_TURN = 4
FOX_TILES = 3 * HEADS_A_TURN
DN_TILES = 6
GATE_TILES = 4
MERGE_TILES = 5
OUT_TILES = 4
DOWN_K = [4, 4, 3] * 4
T_FOX = 0
T_DN = T_FOX + 3 * FH
T_GATE = T_DN + DN_TILES * QKH
T_MERGE = T_GATE + GATE_TILES
T_OUT = T_MERGE + MERGE_TILES * KD - GATE_TILES
T_FFN = T_OUT + OUT_TILES * (D // GROUP)
T_DOWN = T_FFN + 2 * KF
T_END = T_DOWN + len(DOWN_K) * (D // GROUP)
assert not any(n % RAW for n in (T_FOX, T_DN, T_GATE, T_MERGE, T_OUT, T_FFN, T_DOWN, T_END))

AFTER_FOX, AFTER_DN, AFTER_MERGE, AFTER_OUT, AFTER_FFN, AFTER_DOWN = range(1, 7)


def build(nc, x, c, w_ada, b_ada, norm_gains, w_in, dn_conv, dn_a_log, dn_dt_bias, dn_norm_w,
          fox_f_bias, w_branch_dn, w_branch_fox, w_out, w_gate, w_up, w_down, out):
    def by_k(w):
        return w[0].rearrange("(k p) n -> p k n", p=P)

    ada_d, in_d, bdn_d, bfx_d, out_d, gate_d, up_d, down_d = map(
        by_k, (w_ada, w_in, w_branch_dn, w_branch_fox, w_out, w_gate, w_up, w_down))
    x_d = x[0].rearrange("(t p) d -> p t d", p=P)
    y_d = out[0].rearrange("(t p) d -> p t d", p=P)
    conv_d = dn_conv[0].rearrange("(b p) j -> p b j", p=P)

    ctx = ExitStack()
    with ctx:
        def sem(name):
            return ctx.enter_context(nc.semaphore(name))

        def sb(stack, name, shape, dt=F32):
            return stack.enter_context(nc.sbuf_tensor(name, shape, dt))

        raw = sb(ctx, "raw", [P, RAW, TILE])
        whi = sb(ctx, "whi", [P, SPLIT, TILE], F32R)
        wlo = sb(ctx, "wlo", [P, SPLIT, TILE], F32R)
        ones = sb(ctx, "ones", [P, P])
        ident = sb(ctx, "ident", [P, P])
        vecT = sb(ctx, "vecT", [P, 128 + 49])
        adaT = sb(ctx, "adaT", [P, 6, KD])
        mod = sb(ctx, "mod", [P, 2, KD])
        gcol = sb(ctx, "gcol", [P, 2, KD])
        eps = sb(ctx, "eps", [P, 1])
        condT = sb(ctx, "condT", [P, KD])
        stat = sb(ctx, "stat", [P, 4, 2, TT])
        gain = {0: vecT[:, 96:112], 2: vecT[:, 112:128], 1: vecT[:, 144:160], 3: vecT[:, 160:176]}
        nwcol = vecT[:, 176:177]
        with ExitStack() as over_hT:
            hT = [sb(over_hT, "hT_hi", [P, KD, T], F32R), sb(over_hT, "hT_lo", [P, KD, T], F32R)]
            with ExitStack() as s:
                oD = sb(s, "oD", [P, VH, T])
                oF = sb(s, "oF", [P, FH, T])
                gd = sb(s, "gd", [P, TT, GATES])
                beta = sb(s, "beta", [P, TT, VH])
                U = sb(s, "U", [P, P])
                ONSL = sb(s, "ONSL", [P, 2, P])
                SL = ONSL[:, 1, :]
                with ExitStack() as a:
                    adar = sb(a, "adar", [P, ADA, TILE])
                    acc = sb(a, "acc", [P, TILE])
                    wsm = sb(a, "wsm", [P, KD, SMALL])
                    small = sb(a, "small", [P, 6, TT, GATES])
                    praw = sb(a, "praw", [P, TT, SMALL])
                    rows = sb(a, "rows", [P, P])
                    rows2 = sb(a, "rows2", [P, P])
                    brow = sb(a, "brow", [1, 2, GATES])
                    bias_b = sb(a, "bias_b", [P, 2, GATES])
                    foxq = sb(a, "foxq", [P, 2, T])
                    foxk = sb(a, "foxk", [P, 2, T])
                    foxv = sb(a, "foxv", [P, TT, GROUP])
                    CM = sb(a, "CM", [P, 3, P])
                    fS = sb(a, "fS", [P, 3, P])
                    fP = sb(a, "fP", [P, 3, P])
                    fPT = sb(a, "fPT", [P, 3, P])
                    fL = sb(a, "fL", [P, 2, 3, P])
                    lfh = sb(a, "lfh", [P, TT, HEADS_A_TURN])
                    fmax = sb(a, "fmax", [P, 2])
                    fneg = sb(a, "fneg", [P, 2])
                    fsum = sb(a, "fsum", [P, 2])
                    finv = sb(a, "finv", [P, 2])
                with ExitStack() as a:
                    qk = sb(a, "qk", [P, 2, 2, T])
                    vc = sb(a, "vc", [P, 2, 2, T])
                    zc = sb(a, "zc", [P, 2, 2, T])
                    cacc = sb(a, "cacc", [P, 2, T])
                    cw = sb(a, "cw", [P, 2, 4, CONV_K])
                    gh = sb(a, "gh", [P, TT, 2])
                    bh = sb(a, "bh", [P, TT, 2])
                    on = sb(a, "on", [P, 2, T])
                    sq = sb(a, "sq", [P, 2, T])
                    rn = sb(a, "rn", [P, 2, T])
                    rno = sb(a, "rno", [P, 2, T])
                    SLg = sb(a, "SLg", [P, 2, 2, P])
                    gon = sb(a, "gon", [P, 2, P])
                    E = sb(a, "E", [P, 2, 2, P])
                    Em = sb(a, "Em", [P, 2, 2, P])
                    er = sb(a, "er", [P, 2, P])
                    ktok = sb(a, "ktok", [P, P])
                    vtok = sb(a, "vtok", [P, 2, 2, P])
                    qkg = sb(a, "qkg", [P, 2, 2, P])
                    kd = sb(a, "kd", [P, 2, P])
                    LT = sb(a, "LT", [P, 4, P])
                    LTm = sb(a, "LTm", [P, 2, 4, P])
                    attn = sb(a, "attn", [P, 2, 2, P])
                    XX = sb(a, "XX", [P, 4, 2, P])
                    Y = sb(a, "Y", [P, 4, P])
                    u0 = sb(a, "u0", [P, 2, P])
                    S1 = sb(a, "S1", [P, 2, P])
                    rhs1 = sb(a, "rhs1", [P, 2, P])
                    vn1 = sb(a, "vn1", [P, 2, P])
                    LM = sb(a, "LM", [P, LEVELS, P])
                    adar2 = sb(a, "adar2", [P, 2, 2, ADA_COLS])
                    acc2 = sb(a, "acc2", [P, ADA_COLS])
            with ExitStack() as s:
                oD_lo = sb(s, "oD_lo", [P, VH, T], F32R)
                oF_lo = sb(s, "oF_lo", [P, FH, T], F32R)
                oD_hi = sb(s, "oD_hi", [P, VH, T], F32R)
                oF_hi = sb(s, "oF_hi", [P, FH, T], F32R)
                mF = sb(s, "mF", [P, KD, T])
                gt = sb(s, "gt", [P, 2, 2 * T])
                mt = sb(s, "mt", [P, 2, T])
            with ExitStack() as s:
                mT = [sb(s, "mT_hi", [P, KD, T], F32R), sb(s, "mT_lo", [P, KD, T], F32R)]
                ysb = sb(s, "ysb", [P, TT, D])
                Grow = sb(s, "Grow", [P, D])
                junk = sb(s, "junk", [P, D])
                assert T * (2 * KD) + TT * D + 2 * D <= 2 * KF * T
            with ExitStack() as s:
                h2f = sb(s, "h2f", [P, KD, T])
            with ExitStack() as s:
                guT = [sb(s, "guT_hi", [P, KF, T], F32R), sb(s, "guT_lo", [P, KF, T], F32R)]
                x1 = sb(s, "x1", [P, TT, D])
                sg = sb(s, "sg", [P, 2, T])
                guf = sb(s, "guf", [P, 2, T])
        with ExitStack() as s:
            y2 = sb(s, "y2", [P, TT, D])
            Grow2 = sb(s, "Grow2", [P, D])
            junk2 = sb(s, "junk2", [P, D])
        xs = oD[:, 0:KD, :].rearrange("p (t a) b -> p t (a b)", t=TT)
        hf = oD[:, KD:2 * KD, :]

        bank = [ctx.enter_context(nc.psum_tensor(f"bank{i}", [P, 512], F32)) for i in range(8)]

        raw_landed = [sem(f"raw_landed{i}") for i in range(RAW)]
        hi_done, lo_done, tile_used = sem("hi_done"), sem("lo_done"), sem("tile_used")
        ada_landed = [sem(f"ada_landed{i}") for i in range(ADA)]
        ada_used, ada_summed, ada_biased = sem("ada_used"), sem("ada_summed"), sem("ada_biased")
        ada2_landed = [sem("ada2_landed0"), sem("ada2_landed1")]
        ada2_scaled, ada2_used, ada2_summed, ada2_biased = map(sem, (
            "ada2_scaled", "ada2_used", "ada2_summed", "ada2_biased"))
        phase_over = sem("phase_over")
        rows_landed, x_landed, wsm_landed, brow_landed = map(sem, (
            "rows_landed", "x_landed", "wsm_landed", "brow_landed"))
        made, zeroed = sem("made"), sem("zeroed")
        rows_turned, cond_ready, x_squared, x_scaled, x_turned, xT_ready = map(sem, (
            "rows_turned", "cond_ready", "x_squared", "x_scaled", "x_turned", "xT_ready"))
        mod_ready, h_ready, h_hi, h_lo, small_summed, small_read = map(sem, (
            "mod_ready", "h_ready", "h_hi", "h_lo", "small_summed", "small_read"))
        small_v, small_s, decays_ready = sem("small_v"), sem("small_s"), sem("decays_ready")
        q_taken, k_taken, v_taken = map(sem, ("q_taken", "k_taken", "v_taken"))
        lf_picked, fL_ready, scores_made, scores_masked, max_made, neg_made, exp_made = map(sem, (
            "lf_picked", "fL_ready", "scores_made", "scores_masked", "max_made", "neg_made", "exp_made"))
        inv_made, probs_ready, probs_turned, probsT_ready, pv_made, pv_taken = map(sem, (
            "inv_made", "probs_ready", "probs_turned", "probsT_ready", "pv_made", "pv_taken"))
        conv_first, conv_added, conv_read, conv_done, z_read, gates_picked = map(sem, (
            "conv_first", "conv_added", "conv_read", "conv_done", "z_read", "gates_picked"))
        cw_landed = [sem("cw_landed0"), sem("cw_landed1")]
        sq_ready, norms_summed, norms_read, rn_ready, qkn_ready = map(sem, (
            "sq_ready", "norms_summed", "norms_read", "rn_ready", "qkn_ready"))
        SLg_ready, expo_made, E_ready, erow_made, er_ready, Em_ready, qkg_ready, kd_ready = map(sem, (
            "SLg_ready", "expo_made", "E_ready", "erow_made", "er_ready", "Em_ready", "qkg_ready", "kd_ready"))
        v_turned, vtok_ready, k_turned, ktok_ready, dots_made, LT_ready, attn_ready = map(sem, (
            "v_turned", "vtok_ready", "k_turned", "ktok_ready", "dots_made", "LT_ready", "attn_ready"))
        L1_ready, LTm_ready, X_turned, X_ready, Y_made, Y_ready, XY_made = map(sem, (
            "L1_ready", "LTm_ready", "X_turned", "X_ready", "Y_made", "Y_ready", "XY_made"))
        u0_made, u0_ready, S_made, S_ready, R_made, rhs_ready, vn_made, vn_ready, o_made = map(sem, (
            "u0_made", "u0_ready", "S_made", "S_ready", "R_made", "rhs_ready", "vn_made", "vn_ready", "o_made"))
        osq_ready, osum_made, osum_read, orn_ready, o_normed, oD_ready = map(sem, (
            "osq_ready", "osum_made", "osum_read", "orn_ready", "o_normed", "oD_ready"))
        mod2_ready, o_hi, o_lo, gates_ready, part_made, merged, m_hi, m_lo = map(sem, (
            "mod2_ready", "o_hi", "o_lo", "gates_ready", "part_made", "merged", "m_hi", "m_lo"))
        y_taken = [sem("y_taken0"), sem("y_taken1")]
        grow_made, grow_taken = map(sem, ("grow_made", "grow_taken"))
        x1_landed, r_act, r_dve, h2_turned, h2_mod_act, h2_mod_dve, h2_hi, h2_lo = map(sem, (
            "x1_landed", "r_act", "r_dve", "h2_turned", "h2_mod_act", "h2_mod_dve", "h2_hi", "h2_lo"))
        silu_made, gu_mixed, gu_hi, gu_lo = map(sem, ("silu_made", "gu_mixed", "gu_hi", "gu_lo"))
        down_taken = [sem("down_taken0"), sem("down_taken1")]
        grow2_made, grow2_taken, f_act, f_dve, stored = map(sem, (
            "grow2_made", "grow2_taken", "f_act", "f_dve", "stored"))

        block = ctx.enter_context(nc.Block())

        def load_tile(sp, n, src, dyn=0):
            k, cols = src.shape[1], src.shape[2]
            if n >= RAW:
                sp.wait_ge(lo_done, 4 * (n - RAW) + 4 + dyn * 4)
            sp.dma_start(raw[:, n % RAW, 0:k * cols].rearrange("p (k n) -> p k n", k=k), src)\
                .then_inc(raw_landed[n % RAW], 16)

        def split_hi(act, n, dyn=0, size=TILE, parts=HALVES):
            if parts[0][0] == 0:
                act.wait_ge(raw_landed[n % RAW], dyn * (16 // RAW) + 16 * (n // RAW + 1))
                if n >= SPLIT or not isinstance(dyn, int):
                    used(act, n - SPLIT, dyn)
            for a, b in parts:
                at = slice(a * TILE // 4, min(b * TILE // 4, size))
                nc.scalar.activation(whi[:, n % SPLIT, at], raw[:, n % RAW, at], ACT.Copy).then_inc(hi_done, b - a)

        def split_lo(dve, n, dyn=0, size=TILE, parts=HALVES):
            for a, b in parts:
                dve.wait_ge(hi_done, dyn * 4 + 4 * n + b)
                at = slice(a * TILE // 4, min(b * TILE // 4, size))
                nc.vector.tensor_tensor(wlo[:, n % SPLIT, at], raw[:, n % RAW, at],
                                        whi[:, n % SPLIT, at].bitcast(F32), ALU.subtract).then_inc(lo_done, b - a)

        def tile_ready(pe, n, dyn=0, quarters=4):
            pe.wait_ge(lo_done, dyn * 4 + 4 * n + quarters)

        def used(eng, n, dyn=0):
            eng.wait_ge(tile_used, dyn + n + 1)

        def by_channel(pe, dst, n, dyn, acts, ks, first, last, k0=0):
            hi, lo = acts
            step = min(8, len(ks))
            for k in ks:
                if k % step == 0:
                    tile_ready(pe, n, dyn, (k + step) // 4)
                w_hi = whi[:, n % SPLIT, k * P:(k + 1) * P]
                w_lo = wlo[:, n % SPLIT, k * P:(k + 1) * P]
                nc.tensor.matmul(dst, w_hi, hi[:, k0 + k, :], start=first and k == ks[0], stop=False)
                nc.tensor.matmul(dst, w_hi, lo[:, k0 + k, :], start=False, stop=False)
                mm = nc.tensor.matmul(dst, w_lo, hi[:, k0 + k, :], start=False, stop=last and k == ks[-1])
            return mm

        def by_token(pe, dsts, n, dyn, acts, k0, nk, first, last):
            hi, lo = acts
            for k in range(nk):
                if k % 2 == 0:
                    tile_ready(pe, n, dyn, k + 2)
                w_hi = whi[:, n % SPLIT, k * GROUP:(k + 1) * GROUP]
                w_lo = wlo[:, n % SPLIT, k * GROUP:(k + 1) * GROUP]
                for t in range(TT):
                    at = slice(t * P, (t + 1) * P)
                    nc.tensor.matmul(dsts[t][:, :], hi[:, k0 + k, at], w_hi, start=first and k == 0, stop=False)
                    nc.tensor.matmul(dsts[t][:, :], hi[:, k0 + k, at], w_lo, start=False, stop=False)
                    mm = nc.tensor.matmul(dsts[t][:, :], lo[:, k0 + k, at], w_hi, start=False,
                                          stop=last and k == nk - 1)
            return mm

        def meet(eng, n):
            eng.drain().then_inc(phase_over, 1)
            eng.wait_ge(phase_over, 4 * n)

        def load_ada(sp, a, src, dyn=0):
            if a >= ADA:
                sp.wait_ge(ada_used, dyn + a - ADA + 1)
            sp.dma_start(adar[:, a % ADA, :], src).then_inc(ada_landed[a % ADA], 16)

        def add_ada(dve, a, dyn=0, group=0):
            k = a % KD
            dve.wait_ge(ada_landed[a % ADA], dyn * (16 // ADA) + 16 * (a // ADA + 1))
            if k == 0:
                if a:
                    dve.wait_ge(ada_summed, group)
                ins = nc.vector.tensor_scalar(acc[:, :], adar[:, a % ADA, :], condT[:, 0:1], None, ALU.mult)
            else:
                dve.wait_ge(ada_used, dyn + a)
                ins = nc.vector.scalar_tensor_tensor(acc[:, :], adar[:, a % ADA, :], condT[:, k:k + 1], acc[:, :],
                                                     ALU.mult, ALU.add)
            ins.then_inc(ada_used, 1)

        def sum_ada(pe, dst, done):
            pe.wait_ge(ada_used, done)
            for k in range(KD):
                ins = nc.tensor.matmul(dst[:, k:k + 1], acc[:, k * P:(k + 1) * P], ones[:, 0:1], start=True, stop=True)
            ins.then_inc(ada_summed, 1)

        def load_ada2(sp, j, a):
            if not isinstance(j, int) or j > 0 or a >= 2:
                sp.wait_ge(ada2_used, j * (KD - 1) + {0: -2, 1: 0}.get(a, 2 * a - 3))
            sp.dma_start(adar2[:, a % 2, :, :], ada_d[:, 2 * a:2 * a + 2, bass.ds(j * ADA_COLS + 2 * D, ADA_COLS)])\
                .then_inc(ada2_landed[a % 2], 16)

        def scale_ada2(act, j, k, first):
            a, b = divmod(k, 2)
            if b == 0:
                act.wait_ge(ada2_landed[a % 2], j * (16 * ADA_PIECES // 2) + 16 * (a // 2 + 1))
            if k == 0 and not first:
                act.wait_ge(ada2_summed, j)
            at = adar2[:, a % 2, b, :]
            nc.scalar.activation(at if k else acc2[:, :], at, ACT.Copy, scale=condT[:, k:k + 1]).then_inc(ada2_scaled, 1)

        def sum_ada2(pool, j, k):
            a, b = divmod(k, 2)
            pool.wait_ge(ada2_scaled, j * KD + k + 1)
            if k > 1:
                pool.wait_ge(ada2_used, j * (KD - 1) + k - 1)
            nc.gpsimd.tensor_tensor(acc2[:, :], acc2[:, :], adar2[:, a % 2, b, :], ALU.add).then_inc(ada2_used, 1)

        TURNS = FH // HEADS_A_TURN

        def fox_src(i, t):
            if t < 4:
                return in_d[:, 4 * t:4 * t + 4, bass.ds(i * GROUP + (OFF_FOX + 2 * FOX), GROUP)]
            j, which = divmod(t - 4, 2)
            return in_d[:, :, bass.ds(i * GROUP + (OFF_FOX + which * FOX + j * P), P)]

        def dn_col(h, b):
            step, base = ((P, 0), (P, QK_DIM), (2 * P, 2 * QK_DIM), (2 * P, 2 * QK_DIM + P),
                          (2 * P, OFF_Z), (2 * P, OFF_Z + P))[b]
            return h * step + base

        @block.sync
        def _(sp):
            for dst, src in ((rows[0:96, :], b_ada[0].rearrange("(r n) -> r n", n=P)),
                             (rows[96:112, :], norm_gains[0, 0].rearrange("(r n) -> r n", n=P)),
                             (rows[112:128, :], norm_gains[0, 2].rearrange("(r n) -> r n", n=P)),
                             (rows2[0:16, :], c[0].rearrange("(r n) -> r n", n=P)),
                             (rows2[16:32, :], norm_gains[0, 1].rearrange("(r n) -> r n", n=P)),
                             (rows2[32:48, :], norm_gains[0, 3].rearrange("(r n) -> r n", n=P)),
                             (rows2[48:49, :], dn_norm_w)):
                sp.dma_start(dst, src).then_inc(rows_landed, 16)
            for a in range(ADA):
                load_ada(sp, a, ada_d[:, a, 0:D])
            sp.dma_start(xs, x_d).then_inc(x_landed, 16)
            sp.dma_start(brow[0:1, 0, 0:VH], dn_dt_bias).then_inc(brow_landed, 16)
            sp.dma_start(brow[0:1, 0, VH:GATES], fox_f_bias).then_inc(brow_landed, 16)
            sp.dma_start(brow[0:1, 1, 0:VH], dn_a_log).then_inc(brow_landed, 16)
            sp.dma_start(wsm[:, :, 0:2 * VH], in_d[:, :, OFF_B:OFF_FOX]).then_inc(wsm_landed, 16)
            sp.dma_start(wsm[:, :, 2 * VH:SMALL], in_d[:, :, OFF_F:OFF_M]).then_inc(wsm_landed, 16)
            for a in range(ADA, 2 * KD):
                load_ada(sp, a, ada_d[:, a % KD, (a // KD) * D:(a // KD + 1) * D])
            for n in range(RAW):
                load_tile(sp, T_FOX + n, fox_src(0, n))

            def fox_loads(i, loads):
                for n in range(RAW, RAW + loads):
                    src = fox_src(i, n) if n < FOX_TILES else fox_src(i + 1, n - FOX_TILES)
                    load_tile(sp, T_FOX + n, src, i * FOX_TILES)

            with sp.Fori(0, TURNS - 1) as i:
                fox_loads(i, FOX_TILES)
            fox_loads(TURNS - 1, FOX_TILES - RAW)

            def load_cw(h, pr):
                for b, (row, nb) in enumerate(((h, 1), (h + QKH, 1), (h * 2 + 2 * QKH, 2))):
                    sp.dma_start(cw[:, pr, b:b + nb, :], conv_d[:, bass.ds(row, nb), :]).then_inc(cw_landed[pr], 16)

            def dn_tile(n, h, b, dyn=0):
                load_tile(sp, n, in_d[:, :, bass.ds(dn_col(h, b), P)], dyn)

            def gate_src(blk, w):
                return in_d[:, :, bass.ds(blk * P + (OFF_M + w * D), P)]

            def dn_loads(j, pr, n0, dyn, more):
                if more:
                    sp.wait_ge(conv_read, j * 4 + 4)
                    load_cw(j + 2, pr)
                ada_pieces = {0: (), 1: (), 2: (2, 3), 3: (4, 5, 6, 7), 4: (8,), 5: (9,)}
                for b in range(DN_TILES):
                    for a in ada_pieces[b]:
                        load_ada2(sp, j + a // ADA_PIECES, a % ADA_PIECES)
                    if b < DN_TILES - RAW:
                        dn_tile(n0 + RAW + b, j + 1, RAW + b, dyn)
                    elif more:
                        dn_tile(n0 + RAW + b, j + 2, b - (DN_TILES - RAW), dyn)
                    else:
                        load_tile(sp, n0 + RAW + b, gate_src(*divmod(b - (DN_TILES - RAW), 2)))

            for n in range(DN_TILES + RAW):
                if n == RAW:
                    sp.wait_ge(phase_over, 4 * AFTER_FOX)
                    load_cw(0, 0)
                    load_cw(1, 1)
                dn_tile(T_DN + n, n // DN_TILES, n % DN_TILES)
            load_ada2(sp, 0, 0)
            load_ada2(sp, 0, 1)
            dn_loads(0, 0, T_DN + DN_TILES, 0, True)
            with sp.Fori(0, QKH // 2 - 2) as i:
                dn_loads(i * 2 + 1, 1, T_DN + 2 * DN_TILES, i * (2 * DN_TILES), True)
                dn_loads(i * 2 + 2, 0, T_DN + 3 * DN_TILES, i * (2 * DN_TILES), True)
            dn_loads(QKH - 3, 1, T_DN + (QKH - 2) * DN_TILES, 0, True)
            dn_loads(QKH - 2, 0, T_DN + (QKH - 1) * DN_TILES, 0, False)
            def merge_src(i, m):
                sizes = [MERGE_TILES] * 4 if not isinstance(i, int) or i < KD // 4 - 1 else [MERGE_TILES] * 2 + [3] * 2
                b = 0
                while m >= sizes[b]:
                    m, b = m - sizes[b], b + 1
                if m >= 3:
                    return in_d[:, :, bass.ds(i * (4 * P) + (OFF_M + (m - 3) * D + (b + 2) * P), P)]
                w = (bdn_d[:, 0:KD, :], bdn_d[:, KD:2 * KD, :], bfx_d)[m]
                return w.rearrange("p k (b n) -> p k b n", n=P)[:, :, bass.ds(i * 4 + b, 1), :]\
                    .rearrange("p k b n -> p k (b n)")

            def merge_loads(i, loads):
                for m in range(RAW, RAW + loads):
                    src = merge_src(i, m) if m < 4 * MERGE_TILES else merge_src(i + 1, m - 4 * MERGE_TILES)
                    load_tile(sp, T_MERGE + m, src, i * (4 * MERGE_TILES))

            for m in range(RAW):
                if m == RAW - 1:
                    load_ada2(sp, QKH - 1, 2)
                    load_ada2(sp, QKH - 1, 3)
                load_tile(sp, T_MERGE + m, merge_src(0, m))
            for a in range(4, ADA_PIECES):
                load_ada2(sp, QKH - 1, a)
            with sp.Fori(0, KD // 4 - 1) as i:
                merge_loads(i, 4 * MERGE_TILES)
            merge_loads(KD // 4 - 1, 4 * MERGE_TILES - GATE_TILES - RAW)
            with sp.Fori(0, D // GROUP // 2) as i:
                for t in range(2 * OUT_TILES):
                    g, k = divmod(t, OUT_TILES)
                    load_tile(sp, T_OUT + t, out_d[:, 4 * k:4 * k + 4, bass.ds(i * (2 * GROUP) + g * GROUP, GROUP)],
                              i * (2 * OUT_TILES))
            sp.wait_ge(m_lo, 4)
            sp.dma_start(x1[:, :, :], x_d).then_inc(x1_landed, 16)
            with sp.Fori(0, KF // 2) as i:
                for b in range(2):
                    for w, src in enumerate((gate_d, up_d)):
                        load_tile(sp, T_FFN + 2 * b + w, src[:, :, bass.ds(i * (2 * P) + b * P, P)], i * 4)
            with sp.Fori(0, D // GROUP // 2) as i:
                for g in range(2):
                    for t, nk in enumerate(DOWN_K):
                        k = sum(DOWN_K[:t])
                        load_tile(sp, T_DOWN + g * len(DOWN_K) + t,
                                  down_d[:, k:k + nk, bass.ds(i * (2 * GROUP) + g * GROUP, GROUP)],
                                  i * (2 * len(DOWN_K)))
            for t in range(TT):
                sp.wait_ge(f_dve, TT + t + 1)
                sp.dma_start(y_d[:, t, :], x1[:, t, :]).then_inc(stored, 16)
            sp.wait_ge(stored, 16 * TT)

        @block.gpsimd
        def _(pool):
            G = nc.gpsimd
            G.memset(ones[:, :], 1.0).then_inc(made, 1)
            G.memset(eps[:, :], EPS).then_inc(made, 1)
            G.memset(ident[:, :], 0.0).then_inc(zeroed, 1)
            G.memset(U[:, :], 1.0).then_inc(zeroed, 1)
            G.memset(ONSL[:, :, :], 1.0).then_inc(zeroed, 1)
            G.memset(CM[:, :, :], 0.0).then_inc(zeroed, 1)
            pool.wait_ge(zeroed, 4)
            G.affine_select(out=ident[:, :], in_=ident[:, :], compare_op=ALU.not_equal, fill=1.0, base=0,
                            pattern=[[-1, P]], channel_multiplier=1).then_inc(made, 1)
            G.affine_select(out=U[:, :], in_=U[:, :], compare_op=ALU.is_ge, fill=0.0, base=0,
                            pattern=[[1, P]], channel_multiplier=-1).then_inc(made, 1)
            G.affine_select(out=SL, in_=SL, compare_op=ALU.is_gt, fill=0.0, base=0,
                            pattern=[[-1, P]], channel_multiplier=1).then_inc(made, 1)
            G.affine_select(out=CM[:, 1:3, :], in_=CM[:, 1:3, :], compare_op=ALU.is_ge, fill=MASKED, base=0,
                            pattern=[[0, 2], [-1, P]], channel_multiplier=1).then_inc(made, 1)
            pool.wait_ge(made, 6)
            pool.sem_inc(fL_ready, FREE)
            with pool.Fori(0, TURNS) as i:
                pool.wait_ge(lf_picked, i + 1)
                for j in range(HEADS_A_TURN):
                    pool.wait_ge(scores_made, i * HEADS_A_TURN + j + FREE - 1)
                    G.tensor_tensor(fL[:, j % 2, 0, :], U[:, :], lfh[:, 1, j:j + 1].broadcast_to([P, P]), ALU.mult).then_inc(fL_ready, 1)
                    G.tensor_tensor(fL[:, j % 2, 1, :], ones[:, :], lfh[:, 0, j:j + 1].broadcast_to([P, P]), ALU.mult).then_inc(fL_ready, 1)
                    G.tensor_tensor(fL[:, j % 2, 2, :], U[:, :], lfh[:, 0, j:j + 1].broadcast_to([P, P]), ALU.mult).then_inc(fL_ready, 1)
            meet(pool, AFTER_FOX)

            G.memset(LM[:, :, :], 0.0).then_inc(zeroed, 1)
            pool.wait_ge(zeroed, 5)

            def level(v):
                m = 1 << v
                return m, P // (2 * m), LM[:, v, :].rearrange("p (b h r) -> p b h r", h=2, r=m)[:, :, 1, :]

            for v in range(LEVELS):
                m, nb, at = level(v)
                G.memset(at, 1.0).then_inc(zeroed, 1)
            pool.wait_ge(zeroed, 5 + LEVELS)
            for v in range(LEVELS):
                m, nb, at = level(v)
                G.affine_select(out=at, in_=at, compare_op=ALU.is_ge, fill=0.0, base=0,
                                pattern=[[-2 * m, nb], [0, m]], channel_multiplier=1).then_inc(zeroed, 1)
            pool.wait_ge(zeroed, 5 + 2 * LEVELS)
            for v in range(LEVELS):
                m, nb, at = level(v)
                G.affine_select(out=at, in_=at, compare_op=ALU.is_ge, fill=0.0, base=m - 1,
                                pattern=[[2 * m, nb], [0, m]], channel_multiplier=-1).then_inc(made, 1)
            pool.wait_ge(made, 6 + LEVELS)

            def gate_output(h, pr):
                pool.wait_ge(o_normed, h + FREE + 1)
                G.tensor_tensor(oD[:, bass.ds(h * 2, 2), :], on[:, :, :], zc[:, pr, :, :], ALU.mult).then_inc(oD_ready, 1)

            pool.sem_inc(oD_ready, FREE)

            def delta(j, pr, first=False):
                pool.wait_ge(gates_picked, j * 2 + 2)
                if not first:
                    pool.wait_ge(erow_made, j)
                for v in range(2):
                    for ch in range(TT):
                        G.tensor_tensor(SLg[:, v, ch, :], SL, gh[:, ch, v:v + 1].broadcast_to([P, P]), ALU.mult).then_inc(SLg_ready, 1)
                for v in range(2):
                    G.tensor_tensor(gon[:, v, :], ones[:, :], gh[:, 1, v:v + 1].broadcast_to([P, P]), ALU.mult).then_inc(SLg_ready, 1)
                pool.wait_ge(E_ready, j + 1)
                if not first:
                    pool.wait_ge(attn_ready, j * 2)
                G.tensor_tensor(Em[:, :, :, :].rearrange("p a b n -> p (a b) n"),
                                E[:, :, :, :].rearrange("p a b n -> p (a b) n"),
                                U[:, :].unsqueeze(1).broadcast_to([P, 4, P]), ALU.mult).then_inc(Em_ready, 1)
                pool.wait_ge(qkn_ready, j * 2 + 2)
                pool.wait_ge(er_ready, j + 1)
                if not first:
                    pool.wait_ge(o_made, j)
                for v in range(2):
                    G.tensor_tensor(qkg[:, v, :, :], qk[:, pr, :, P:T],
                                    er[:, v, :].unsqueeze(1).broadcast_to([P, 2, P]), ALU.mult).then_inc(qkg_ready, 1)
                if not first:
                    gate_output(j - 1, 1 - pr)
                pool.wait_ge(LT_ready, j * 4 + 4)
                for v in range(1, LEVELS):
                    if v >= 3:
                        pool.wait_ge(Y_made, j * 24 + 4 * (v - 2))
                    elif not first:
                        pool.wait_ge(Y_made, j * 24)
                    G.tensor_tensor(LTm[:, v % 2, :, :], LT[:, :, :], LM[:, v:v + 1, :].broadcast_to([P, 4, P]),
                                    ALU.mult).then_inc(LTm_ready, 1)
                    for k in range(2 * v - 5, 2 * v - 3):
                        if k > 0:
                            sum_ada2(pool, j, k)
                pool.wait_ge(ktok_ready, j + 1)
                if not first:
                    pool.wait_ge(S_made, j)
                for v in range(2):
                    G.tensor_tensor(kd[:, v, :], ktok[:, :], E[:, 0, v, P - 1:P].broadcast_to([P, P]), ALU.mult).then_inc(kd_ready, 1)
                for k in range(2 * LEVELS - 5, KD):
                    sum_ada2(pool, j, k)

            delta(0, 0, True)
            with pool.Fori(0, QKH // 2 - 1) as i:
                delta(i * 2 + 1, 1)
                delta(i * 2 + 2, 0)
            delta(QKH - 1, 1)
            gate_output(QKH - 1, 1)
            for n in (AFTER_DN, AFTER_MERGE, AFTER_OUT, AFTER_FFN, AFTER_DOWN):
                meet(pool, n)

        @block.scalar
        def _(act):
            A = nc.scalar.activation

            def ln_exp():
                act.preload_act_table_set("natural_log_exp_and_others")

            def silu():
                act.preload_act_table(ACT.Silu)

            def rms(n, src, scratch, done, base):
                total, inverse = stat[:, n, 0, :], stat[:, n, 1, :]
                for t in range(TT):
                    A(scratch, src[:, t, :], ACT.Square, accum_out=total[:, t:t + 1]).then_inc(done, 1)
                    act.wait_ge(done, base + t + 1)
                A(inverse, total, ACT.Ln, bias=eps[:, 0:1], scale=1.0 / D).then_inc(done, 1)
                act.wait_ge(done, base + TT + 1)
                A(inverse, inverse, ACT.Exp, scale=-0.5).then_inc(done, 1)

            silu()
            act.wait_ge(made, 6)
            act.wait_ge(rows_turned, 1)
            A(vecT[:, :], bank[0][:, 0:177], ACT.Copy).then_inc(cond_ready, 1)
            A(condT[:, :], bank[0][:, 128:144], ACT.Silu).then_inc(cond_ready, 1)
            ln_exp()
            act.wait_ge(x_landed, 16)
            rms(0, xs, hf.rearrange("p a b -> p (a b)")[:, 0:D], x_squared, 0)
            for g in range(8):
                act.wait_ge(x_turned, g + 1)
                A(hf[:, 2 * g:2 * g + 2, :], bank[1 + g % 4][:, :].rearrange("p (a b) -> p a b", a=2),
                  ACT.Copy).then_inc(xT_ready, 1)
            split_hi(act, T_FOX)
            for g in range(4):
                act.wait_ge(h_ready, 4 * g + 4)
                A(hT[0][:, 4 * g:4 * g + 4, :], hf[:, 4 * g:4 * g + 4, :], ACT.Copy).then_inc(h_hi, 1)
            act.preload_act_table(ACT.Sigmoid)
            act.wait_ge(small_summed, 1)
            A(praw[:, :, :].rearrange("p t n -> p (t n)"), bank[7][:, 0:TT * SMALL], ACT.Copy).then_inc(small_read, 1)
            A(bias_b[:, :, :].rearrange("p t n -> p (t n)"), bank[7][:, 256:256 + 2 * GATES], ACT.Copy).then_inc(small_read, 1)
            act.wait_ge(small_read, 2)
            A(beta[:, :, :], praw[:, :, 0:VH], ACT.Sigmoid).then_inc(small_s, 1)
            ln_exp()
            A(small[:, 5, 0, 0:VH], bias_b[:, 1, 0:VH], ACT.Exp).then_inc(small_s, 1)
            act.wait_ge(small_v, 6)
            A(small[:, 2, :, :], small[:, 1, :, :], ACT.Exp).then_inc(small_s, 1)
            act.wait_ge(small_s, 3)
            A(small[:, 3, :, :], small[:, 2, :, :], ACT.Ln, bias=ones[:, 0:1]).then_inc(small_s, 1)

            for s in (q_taken, k_taken, v_taken, exp_made, probsT_ready, pv_taken):
                act.sem_inc(s, FREE)

            def fox_take(h, j, which, n, dyn):
                taken, dst = ((q_taken, foxq), (k_taken, foxk))[which]
                used(act, n, dyn)
                act.wait_ge(scores_made, h + FREE - 1)
                A(dst[:, j % 2, :], bank[2 + which][:, 0:T], ACT.Copy).then_inc(taken, 1)

            def fox_exps(h):
                act.wait_ge(neg_made, h + 1)
                act.wait_ge(probs_turned, h + FREE)
                A(fP[:, 0:2, :], fS[:, 0:2, :], ACT.Exp, bias=fneg[:, 1:2], scale=SCALE,
                  accum_out=fsum[:, 1:2]).then_inc(exp_made, 1)
                A(fP[:, 2, :], fS[:, 2, :], ACT.Exp, bias=fneg[:, 0:1], scale=SCALE,
                  accum_out=fsum[:, 0:1]).then_inc(exp_made, 1)

            def fox_probsT(h):
                act.wait_ge(probs_turned, h + FREE + 1)
                act.wait_ge(pv_made, h + FREE)
                A(fPT[:, :, :].rearrange("p a b -> p (a b)"), bank[5][:, 0:3 * P], ACT.Copy).then_inc(probsT_ready, 1)

            def fox_o(h):
                act.wait_ge(pv_made, h + FREE + 1)
                A(oF[:, bass.ds(h, 1), :], bank[6][:, 0:T].unsqueeze(1), ACT.Copy).then_inc(pv_taken, 1)

            def fox_turn(i, first):
                dyn, h = i * FOX_TILES, i * HEADS_A_TURN
                for t in range(FOX_TILES):
                    split_hi(act, T_FOX + t + 1, dyn)
                    if t == 0 and not first:
                        fox_take(h - 1, HEADS_A_TURN - 1, 1, T_FOX - 1, dyn)
                        fox_probsT(h - 2)
                    if t == 1 and not first:
                        fox_o(h - 2)
                        fox_exps(h - 1)
                    if t == 2 and not first:
                        fox_probsT(h - 1)
                    if t == 3 and not first:
                        fox_o(h - 1)
                    if t == 4:
                        used(act, T_FOX + 3, dyn)
                        act.wait_ge(pv_made, h + FREE)
                        for tt in range(TT):
                            A(foxv[:, tt, :], bank[tt][:, :], ACT.Copy).then_inc(v_taken, 1)
                    if t >= 5:
                        j, which = divmod(t - 5, 2)
                        fox_take(h + j, j, which, T_FOX + t - 1, dyn)
                    if t in (7, 9, 11):
                        fox_exps(h + (t - 7) // 2)
                    if t in (8, 10):
                        fox_probsT(h + (t - 8) // 2)
                    if t in (9, 11):
                        fox_o(h + (t - 9) // 2)

            fox_turn(0, True)
            with act.Fori(1, TURNS) as i:
                fox_turn(i, False)
            fox_take(FH - 1, HEADS_A_TURN - 1, 1, T_DN - 1, 0)
            fox_probsT(FH - 2)
            fox_o(FH - 2)
            fox_exps(FH - 1)
            fox_probsT(FH - 1)
            fox_o(FH - 1)
            meet(act, AFTER_FOX)

            def conv_tap(h, b, pr, h2):
                used(act, T_DN + b, h * DN_TILES)
                if b == 0:
                    act.wait_ge(cw_landed[pr], h2 * 48 + 48)
                if b >= 2 or not (isinstance(h, int) and h == 0):
                    act.wait_ge(conv_done, h * 4 + (b - 1))
                A(cacc[:, b % 2, :], bank[b % 2][:, 0:T], ACT.Copy, scale=cw[:, pr, b, 3:4]).then_inc(conv_first, 1)

            def conv_silu(h, b, pr):
                act.wait_ge(conv_read, h * 4 + (b + 1))
                A(qk[:, pr, b, :] if b < 2 else vc[:, pr, b - 2, :], cacc[:, b % 2, :], ACT.Silu).then_inc(conv_done, 1)

            act.sem_inc(o_normed, FREE)

            def z_silu(h, b, pr):
                used(act, T_DN + 4 + b, h * DN_TILES)
                if not isinstance(h, int) or h >= 2:
                    act.wait_ge(oD_ready, h + FREE - 1)
                A(zc[:, pr, b, :], bank[b][:, 0:T], ACT.Silu).then_inc(z_read, 1)

            def step(j, pr, j2, n0, dyn, first=False, project=True, tiles=DN_TILES):
                for s in range(SLOTS):
                    for q in RUNS[s]:
                        if q < 4 * tiles:
                            split_hi(act, n0 + q // 4 + 1, dyn, TILE, ((q % 4, q % 4 + 1),))
                    if s in ADA_SLOTS:
                        scale_ada2(act, j, ADA_SLOTS.index(s), first)
                    if s == 4:
                        silu()
                    if s == 0:
                        z_silu(j, 1, pr)
                        act.wait_ge(conv_done, j * 4 + 2)
                        if not first:
                            act.wait_ge(osum_made, j)
                        A(sq[:, :, :], qk[:, pr, :, :], ACT.Square).then_inc(sq_ready, 1)
                    if s == 1:
                        ln_exp()
                        if not first:
                            act.wait_ge(o_normed, j + FREE - 1)
                            act.wait_ge(osum_made, j)
                            A(rno[:, :, :].rearrange("p a b -> p (a b)"), bank[5][:, :], ACT.Ln, bias=eps[:, 0:1],
                              scale=1.0 / P).then_inc(osum_read, 1)
                        act.wait_ge(norms_summed, j + 1)
                        A(rn[:, :, :].rearrange("p a b -> p (a b)"), bank[2][:, :], ACT.Ln, bias=eps[:, 0:1]).then_inc(norms_read, 1)
                        if not first:
                            act.wait_ge(osum_read, j)
                            A(rno[:, :, :], rno[:, :, :], ACT.Exp, scale=-0.5).then_inc(orn_ready, 1)
                        act.wait_ge(norms_read, j + 1)
                        A(rn[:, :, :], rn[:, :, :], ACT.Exp, scale=-0.5).then_inc(rn_ready, 1)
                        act.wait_ge(expo_made, j + 1)
                        if not first:
                            act.wait_ge(kd_ready, j * 2)
                            act.wait_ge(LT_ready, j * 4)
                        A(E[:, :, :, :].rearrange("p a b n -> p (a b n)"), bank[3][:, :], ACT.Exp).then_inc(E_ready, 1)
                        act.wait_ge(erow_made, j + 1)
                        A(er[:, :, :].rearrange("p a b -> p (a b)"), bank[6][:, 0:T], ACT.Exp).then_inc(er_ready, 1)
                    if s == 2:
                        act.wait_ge(v_turned, j + 1)
                        if not first:
                            act.wait_ge(rhs_ready, j)
                        A(vtok[:, :, :, :].rearrange("p a b n -> p (a b n)"), bank[7][:, :], ACT.Copy).then_inc(vtok_ready, 1)
                    if s == 3:
                        act.wait_ge(k_turned, j + 1)
                        A(ktok[:, :], bank[5][:, 0:P], ACT.Copy).then_inc(ktok_ready, 1)
                    if s in (5, 7, 9, 11, 13, 15):
                        for u in range(4):
                            act.wait_ge(Y_made, j * 24 + (4 * ((s - 5) // 2) + u + 1))
                            A(Y[:, u, :], bank[4 + u][:, 0:P], ACT.Copy).then_inc(Y_ready, 1)
                    if s == 17:
                        act.wait_ge(u0_made, j + 1)
                        for v in range(2):
                            A(u0[:, v, :], bank[2][:, v * P:(v + 1) * P], ACT.Copy, scale=bh[:, 0, v:v + 1]).then_inc(u0_ready, 1)
                    if s == 18:
                        act.wait_ge(S_made, j + 1)
                        A(S1[:, :, :].rearrange("p a b -> p (a b)"), bank[3][:, 0:T], ACT.Copy).then_inc(S_ready, 1)
                    if s == 20:
                        act.wait_ge(vn_made, j + 1)
                        for v in range(2):
                            A(vn1[:, v, :], bank[3][:, T + v * P:T + (v + 1) * P], ACT.Copy,
                              scale=bh[:, 1, v:v + 1]).then_inc(vn_ready, 1)
                    if s == 21:
                        act.wait_ge(o_made, j + 1)
                        A(sq[:, :, :].rearrange("p a b -> p (a b)"), bank[4][:, :], ACT.Square).then_inc(osq_ready, 1)
                    if s == END[4] + 1 and project:
                        z_silu(j + 1, 0, 1 - pr)
                    for b in range(4):
                        if project and s == CONV_SLOTS[b]:
                            conv_tap(j + 1, b, 1 - pr, j2)
                        if project and s == CONV_SLOTS[b] + 2:
                            conv_silu(j + 1, b, 1 - pr)
                    if s == 22 and not project:
                        ln_exp()
                        act.wait_ge(o_normed, j + FREE)
                        act.wait_ge(osum_made, j + 1)
                        A(rno[:, :, :].rearrange("p a b -> p (a b)"), bank[5][:, :], ACT.Ln, bias=eps[:, 0:1],
                          scale=1.0 / P).then_inc(osum_read, 1)
                        act.wait_ge(osum_read, j + 1)
                        A(rno[:, :, :], rno[:, :, :], ACT.Exp, scale=-0.5).then_inc(orn_ready, 1)

            silu()
            for b in range(DN_TILES):
                split_hi(act, T_DN + b + 1)
                if 1 <= b <= 4:
                    conv_tap(0, b - 1, 0, 0)
                    conv_silu(0, b - 1, 0)
                if b == 5:
                    z_silu(0, 0, 0)
            step(0, 0, 0, T_DN + DN_TILES, 0, first=True)
            with act.Fori(0, QKH // 2 - 1) as i:
                step(i * 2 + 1, 1, i + 1, T_DN + 2 * DN_TILES, i * (2 * DN_TILES))
                step(i * 2 + 2, 0, i + 1, T_DN + 3 * DN_TILES, i * (2 * DN_TILES))
            step(QKH - 1, 1, 0, T_GATE, 0, project=False, tiles=GATE_TILES)
            meet(act, AFTER_DN)

            for g in range(12):
                src, dst, k = (oD, oD_hi, 4 * g) if g < 8 else (oF, oF_hi, 4 * (g - 8))
                A(dst[:, k:k + 4, :], src[:, k:k + 4, :], ACT.Copy).then_inc(o_hi, 1)
            act.preload_act_table(ACT.Sigmoid)
            used(act, T_GATE + GATE_TILES - 1)
            for b in range(2):
                A(gt[:, b, :], bank[b][:, :], ACT.Sigmoid).then_inc(gates_ready, 1)

            def merge(i, blocks):
                n, dyn = T_MERGE, i * (4 * MERGE_TILES)
                for b in range(blocks):
                    gates = not isinstance(i, int) or 4 * i + b < KD - 2
                    for t in range(MERGE_TILES if gates else 3):
                        split_hi(act, n + t + 1, dyn)
                    if gates:
                        used(act, n + MERGE_TILES - 1, dyn)
                        act.wait_ge(merged, i * 4 + b + FREE + 1)
                        A(gt[:, b % 2, :], bank[b % 2][:, :], ACT.Sigmoid).then_inc(gates_ready, 1)
                    n += MERGE_TILES if gates else 3

            with act.Fori(0, KD // 4 - 1) as i:
                merge(i, 4)
            merge(KD // 4 - 1, 4)
            meet(act, AFTER_MERGE)
            for g in range(4):
                A(mT[0][:, 4 * g:4 * g + 4, :], mF[:, 4 * g:4 * g + 4, :], ACT.Copy).then_inc(m_hi, 1)

            for g in range(4):
                act.wait_ge(grow_made, 1)
                A(Grow[:, g * GROUP:(g + 1) * GROUP], bank[4 + g][:, :], ACT.Copy).then_inc(grow_taken, 1)
            act.sem_inc(y_taken[0], FREE)
            with act.Fori(0, D // GROUP // 2) as i:
                dyn = i * (2 * OUT_TILES)
                for t in range(2 * OUT_TILES):
                    split_hi(act, T_OUT + t + 1, dyn)
                    if t == OUT_TILES:
                        used(act, T_OUT + OUT_TILES - 1, dyn)
                        A(ysb[:, 0, bass.ds(i * (2 * GROUP), GROUP)], bank[0][:, :], ACT.Copy).then_inc(y_taken[0], 1)
                used(act, T_OUT + 2 * OUT_TILES - 1, dyn)
                A(ysb[:, 0, bass.ds(i * (2 * GROUP) + GROUP, GROUP)], bank[2][:, :], ACT.Copy).then_inc(y_taken[0], 1)
            meet(act, AFTER_OUT)
            ln_exp()
            rms(1, ysb, junk[:, :], r_act, 0)
            act.wait_ge(r_dve, 2 * TT)
            rms(2, x1, junk[:, :], r_act, TT + 2)
            for g in range(1, 8, 2):
                act.wait_ge(h2_turned, g + 1)
                for k in (2 * g, 2 * g + 1):
                    A(h2f[:, k, :], bank[g][:, (k % 2) * T:(k % 2 + 1) * T], ACT.Identity,
                      bias=adaT[:, 3, k:k + 1], scale=mod[:, 1, k:k + 1]).then_inc(h2_mod_act, 1)
            act.wait_ge(h2_mod_act, 8)
            act.wait_ge(h2_mod_dve, 8)
            for g in range(4):
                A(hT[0][:, 4 * g:4 * g + 4, :], h2f[:, 4 * g:4 * g + 4, :], ACT.Copy).then_inc(h2_hi, 1)
            act.wait_ge(h2_lo, 4)
            silu()
            with act.Fori(0, KF // 2) as i:
                dyn = i * 4
                for t in range(4):
                    b, w = divmod(t, 2)
                    split_hi(act, T_FFN + t + 1, dyn)
                    if w == 1:
                        used(act, T_FFN + 2 * b, dyn)
                        act.wait_ge(gu_mixed, i * 2 + b + FREE - 1)
                        A(sg[:, b, :], bank[2 * b][:, 0:T], ACT.Silu).then_inc(silu_made, 1)
                        act.wait_ge(gu_mixed, i * 2 + b + FREE + 1)
                        A(guT[0][:, bass.ds(i * 2 + b, 1), :], guf[:, b:b + 1, :], ACT.Copy).then_inc(gu_hi, 1)
            meet(act, AFTER_FFN)
            for g in range(4):
                act.wait_ge(grow2_made, 1)
                A(Grow2[:, g * GROUP:(g + 1) * GROUP], bank[4 + g][:, :], ACT.Copy).then_inc(grow2_taken, 1)
            act.sem_inc(down_taken[0], FREE)
            nd = len(DOWN_K)

            def down(i, more):
                for t in range(2 * nd):
                    if more or t < 2 * nd - 1:
                        split_hi(act, T_DOWN + t + 1, i * (2 * nd), DOWN_K[(t + 1) % nd] * GROUP)
                    if t == nd:
                        used(act, T_DOWN + nd - 1, i * (2 * nd))
                        A(y2[:, 0, bass.ds(i * (2 * GROUP), GROUP)], bank[0][:, :], ACT.Copy).then_inc(down_taken[0], 1)
                used(act, T_DOWN + 2 * nd - 1, i * (2 * nd))
                A(y2[:, 0, bass.ds(i * (2 * GROUP) + GROUP, GROUP)], bank[2][:, :], ACT.Copy).then_inc(down_taken[0], 1)

            with act.Fori(0, D // GROUP // 2 - 1) as i:
                down(i, True)
            down(D // GROUP // 2 - 1, False)
            meet(act, AFTER_DOWN)
            ln_exp()
            rms(3, y2, junk2[:, :], f_act, 0)

        @block.tensor
        def _(pe):
            mm = nc.tensor.matmul
            tr = nc.tensor.transpose
            for s in (scores_made, pv_made, probs_turned):
                pe.sem_inc(s, FREE)
            pe.wait_ge(made, 6)
            pe.wait_ge(rows_landed, 7 * 16)
            tr(bank[0][:, 0:P], rows[:, :], ident[:, :])
            tr(bank[0][:, P:P + 49], rows2[0:49, :], ident[0:49, 0:49]).then_inc(rows_turned, 1)
            pe.wait_ge(x_scaled, TT)
            for g in range(8):
                if g >= 4:
                    pe.wait_ge(xT_ready, g - 3)
                for k in (2 * g, 2 * g + 1):
                    for t in range(TT):
                        at = (k % 2) * T + t * P
                        ins = tr(bank[1 + g % 4][:, at:at + P], xs[:, t, k * P:(k + 1) * P], ident[:, :])
                ins.then_inc(x_turned, 1)
            pe.wait_ge(cond_ready, 2)
            sum_ada(pe, bank[0], KD)
            pe.wait_ge(ada_biased, 1)
            sum_ada(pe, bank[0], 2 * KD)
            pe.wait_ge(wsm_landed, 32)
            pe.wait_ge(h_ready, KD)
            for t in range(TT):
                for k in range(KD):
                    mm(bank[7][:, t * SMALL:(t + 1) * SMALL], hf[:, k, t * P:(t + 1) * P], wsm[:, k, :],
                       start=(k == 0), stop=(k == KD - 1))
            pe.wait_ge(brow_landed, 48)
            pe.wait_ge(small_v, 1)
            mm(bank[7][:, 256:256 + 2 * GATES], ones[0:1, :], brow[0:1, :, :].rearrange("p a b -> p (a b)"),
               start=True, stop=True).then_inc(small_summed, 1)
            pe.wait_ge(h_lo, 4)

            def fox_scores(h, j):
                s = bank[4]
                pe.wait_ge(q_taken, h + FREE + 1)
                pe.wait_ge(k_taken, h + FREE + 1)
                pe.wait_ge(fL_ready, h * 3 + 3 + FREE)
                pe.wait_ge(scores_masked, h + FREE)
                mm(s[:, 0:T], foxq[:, j % 2, P:T], foxk[:, j % 2, :], start=True, stop=False)
                mm(s[:, 0:P], fL[:, j % 2, 1, :], SL, start=False, stop=False)
                mm(s[:, 0:T], fL[:, j % 2, 0, :], ONSL[:, :, :].rearrange("p a b -> p (a b)"), start=False, stop=True)
                mm(s[:, T:T + P], foxq[:, j % 2, 0:P], foxk[:, j % 2, 0:P], start=True, stop=False)
                mm(s[:, T:T + P], fL[:, j % 2, 2, :], SL, start=False, stop=True).then_inc(scores_made, 1)

            def fox_turn(h):
                pe.wait_ge(probs_ready, h * 2 + 2)
                pe.wait_ge(probsT_ready, h + FREE)
                for n, blk in enumerate((2, 0, 1)):
                    ins = tr(bank[5][:, n * P:(n + 1) * P], fP[:, blk, :], ident[:, :])
                ins.then_inc(probs_turned, 1)

            def fox_pv(h, j):
                pe.wait_ge(probsT_ready, h + FREE + 1)
                pe.wait_ge(pv_taken, h + FREE)
                v = foxv[:, :, j * P:(j + 1) * P]
                mm(bank[6][:, 0:P], v[:, 0, :], fPT[:, 0, :], start=True, stop=True)
                mm(bank[6][:, P:T], v[:, 0, :], fPT[:, 1, :], start=True, stop=False)
                mm(bank[6][:, P:T], v[:, 1, :], fPT[:, 2, :], start=False, stop=True).then_inc(pv_made, 1)

            def fox(i, first):
                dyn, h = i * FOX_TILES, i * HEADS_A_TURN
                for t in range(FOX_TILES):
                    n = T_FOX + t
                    if t < 4:
                        if t == 0:
                            pe.wait_ge(v_taken, i * TT + FREE)
                        ins = by_token(pe, bank[0:2], n, dyn, hT, 4 * t, 4, t == 0, t == 3)
                    else:
                        j, which = divmod(t - 4, 2)
                        pe.wait_ge((q_taken, k_taken)[which], h + j + FREE)
                        ins = by_channel(pe, bank[2 + which][:, 0:T], n, dyn, hT, range(KD), True, True)
                    ins.then_inc(tile_used, 1)
                    if t == 0 and not first:
                        fox_pv(h - 2, 2)
                        fox_scores(h - 1, 3)
                    if t == 1 and not first:
                        fox_turn(h - 1)
                    if t == 2 and not first:
                        fox_pv(h - 1, 3)
                    if t == 6:
                        fox_scores(h, 0)
                    if t == 7:
                        fox_turn(h)
                    if t == 8:
                        pe.wait_ge(v_taken, i * TT + TT + FREE)
                        fox_pv(h, 0)
                        fox_scores(h + 1, 1)
                    if t == 9:
                        fox_turn(h + 1)
                    if t == 10:
                        fox_pv(h + 1, 1)
                        fox_scores(h + 2, 2)
                    if t == 11:
                        fox_turn(h + 2)

            fox(0, True)
            with pe.Fori(1, TURNS) as i:
                fox(i, False)
            fox_pv(FH - 2, 2)
            fox_scores(FH - 1, 3)
            fox_turn(FH - 1)
            fox_pv(FH - 1, 3)
            meet(pe, AFTER_FOX)

            def project(h, b, q, n, dyn, first):
                if q == 0:
                    if b >= 2:
                        pe.wait_ge(conv_read, h * 4 + (b - 1))
                    elif not first:
                        pe.wait_ge(z_read, h * 2 + (b - 1))
                ins = by_channel(pe, bank[b % 2][:, 0:T], n, dyn, hT, range(4 * q, 4 * q + 4), q == 0, q == 3)
                if q == 3:
                    ins.then_inc(tile_used, 1)

            def delta(j, pr, s, first):
                if s == 0:
                    pe.wait_ge(sq_ready, j + 1)
                    if not first:
                        pe.wait_ge(rhs_ready, j)
                    mm(bank[2][:, :], ones[:, :], sq[:, :, :].rearrange("p a b -> p (a b)"), start=True,
                       stop=True).then_inc(norms_summed, 1)
                if s == 1:
                    pe.wait_ge(SLg_ready, j * 6 + 6)
                    if not first:
                        pe.wait_ge(vn_ready, j * 2)
                        pe.wait_ge(X_ready, j * 26)
                    for ch in range(TT):
                        for v in range(2):
                            u = 2 * ch + v
                            ins = mm(bank[3][:, u * P:(u + 1) * P], SLg[:, v, ch, :], U[:, :], start=True, stop=True)
                    ins.then_inc(expo_made, 1)
                    for v in range(2):
                        ins = mm(bank[6][:, v * P:(v + 1) * P], gon[:, v, :], U[:, :], start=True, stop=True)
                    ins.then_inc(erow_made, 1)
                if s == 2:
                    pe.wait_ge(conv_done, j * 4 + 4)
                    if not first:
                        pe.wait_ge(ada2_biased, j)
                    for v in range(2):
                        for ch in range(TT):
                            at = (2 * v + ch) * P
                            ins = tr(bank[7][:, at:at + P], vc[:, pr, v, ch * P:(ch + 1) * P], ident[:, :])
                    ins.then_inc(v_turned, 1)
                if s == 3:
                    pe.wait_ge(qkn_ready, j * 2 + 2)
                    pe.wait_ge(norms_read, j + 1)
                    for ch in range(TT):
                        at = slice(ch * P, (ch + 1) * P)
                        ins = mm(bank[2][:, ch * T:(ch + 1) * T].rearrange("p (a b) -> p a b", a=2), qk[:, pr, 1, at],
                                 qk[:, pr, :, at], start=True, stop=True)
                    ins.then_inc(dots_made, 1)
                    if not first:
                        pe.wait_ge(osum_read, j)
                    tr(bank[5][:, 0:P], qk[:, pr, 1, 0:P], ident[:, :]).then_inc(k_turned, 1)
                if 5 <= s <= 16:
                    v, half = divmod(s - 5, 2)
                    for u in range(4):
                        if half == 0:
                            if v == 0 and u == 0:
                                pe.wait_ge(X_ready, j * 26 + 2)
                                pe.wait_ge(vtok_ready, j + 1)
                                pe.wait_ge(ktok_ready, j + 1)
                                pe.wait_ge(er_ready, j + 1)
                                if not first:
                                    pe.wait_ge(o_normed, j + FREE)
                            if u == 0:
                                pe.wait_ge(LTm_ready, j * 6 + (v + 1))
                            if v > 0:
                                pe.wait_ge(X_ready, j * 26 + (2 + 4 * (v - 1) + u + 1))
                            mm(bank[4 + u][:, 0:P], LTm[:, (v + 1) % 2, u, :], XX[:, u, 0, :], start=True,
                               stop=True).then_inc(Y_made, 1)
                        else:
                            pe.wait_ge(Y_ready, j * 24 + (4 * v + u + 1))
                            if 1 <= v < TRANSPOSED and u == 0:
                                pe.wait_ge(X_turned, j * (TRANSPOSED - 1) + v)
                            last = v + 1 == LEVELS - 1
                            if not last:
                                ins = mm(bank[4 + u][:, P:2 * P], XX[:, u, 1, :], Y[:, u, :], start=True, stop=True)
                            if v + 1 >= TRANSPOSED:
                                ins = mm(bank[4 + u][:, 2 * P:3 * P], Y[:, u, :], XX[:, u, 1, :], start=True, stop=True)
                            ins.then_inc(XY_made, 1)
                if s == 17:
                    pe.wait_ge(X_ready, j * 26 + 26)
                    pe.wait_ge(attn_ready, j * 2 + 2)
                    for v in range(2):
                        ins = mm(bank[2][:, v * P:(v + 1) * P], XX[:, v, 1, :], vtok[:, v, 0, :], start=True, stop=True)
                    ins.then_inc(u0_made, 1)
                if s == 18:
                    pe.wait_ge(u0_ready, j * 2 + 2)
                    pe.wait_ge(kd_ready, j * 2 + 2)
                    for v in range(2):
                        ins = mm(bank[3][:, v * P:(v + 1) * P], kd[:, v, :], u0[:, v, :], start=True, stop=True)
                    ins.then_inc(S_made, 1)
                if s == 19:
                    pe.wait_ge(S_ready, j + 1)
                    pe.wait_ge(qkg_ready, j * 2 + 2)
                    for v in range(2):
                        ins = mm(bank[2][:, T + v * P:T + (v + 1) * P], qkg[:, v, 1, :], S1[:, v, :], start=True, stop=True)
                    ins.then_inc(R_made, 1)
                if s == 20:
                    pe.wait_ge(rhs_ready, j + 1)
                    for v in range(2):
                        ins = mm(bank[3][:, T + v * P:T + (v + 1) * P], XX[:, 2 + v, 1, :], rhs1[:, v, :], start=True, stop=True)
                    ins.then_inc(vn_made, 1)
                if s == 21:
                    pe.wait_ge(vn_ready, j * 2 + 2)
                    for v in range(2):
                        o = bank[4]
                        mm(o[:, v * T:v * T + P], u0[:, v, :], attn[:, 0, v, :], start=True, stop=True)
                        mm(o[:, v * T + P:(v + 1) * T], S1[:, v, :], qkg[:, v, 0, :], start=True, stop=False)
                        ins = mm(o[:, v * T + P:(v + 1) * T], vn1[:, v, :], attn[:, 1, v, :], start=False, stop=True)
                    ins.then_inc(o_made, 1)
                if s == 22:
                    pe.wait_ge(osq_ready, j + 1)
                    mm(bank[5][:, :], ones[:, :], sq[:, :, :].rearrange("p a b -> p (a b)"), start=True,
                       stop=True).then_inc(osum_made, 1)
                if s == 23:
                    pe.wait_ge(ada2_used, j * (KD - 1) + (KD - 1))
                    for k in range(ADA_COLS // P):
                        ins = mm(bank[7][:, k:k + 1], acc2[:, k * P:(k + 1) * P], ones[:, 0:1], start=True, stop=True)
                    ins.then_inc(ada2_summed, 1)

            for b in range(DN_TILES):
                for q in range(4):
                    project(0, b, q, T_DN + b, 0, True)

            def gate_quarter(g, q):
                b, w = divmod(g, 2)
                if w == q == 0:
                    pe.wait_ge(z_read, 2 * (QKH - 1) + b + 1)
                ins = by_channel(pe, bank[b][:, w * T:(w + 1) * T], T_GATE + g, 0, hT, range(4 * q, 4 * q + 4),
                                 q == 0, q == 3)
                if q == 3:
                    ins.then_inc(tile_used, 1)

            def step(j, pr, n0, dyn, first=False, projecting=True):
                for s in range(SLOTS):
                    for q in RUNS[s]:
                        if projecting:
                            project(j + 1, q // 4, q % 4, n0 + q // 4, dyn, False)
                        elif q < 4 * GATE_TILES:
                            gate_quarter(q // 4, q % 4)
                    delta(j, pr, s, first)

            step(0, 0, T_DN + DN_TILES, 0, first=True)
            with pe.Fori(0, QKH // 2 - 1) as i:
                step(i * 2 + 1, 1, T_DN + 2 * DN_TILES, i * (2 * DN_TILES))
                step(i * 2 + 2, 0, T_DN + 3 * DN_TILES, i * (2 * DN_TILES))
            step(QKH - 1, 1, 0, 0, projecting=False)
            meet(pe, AFTER_DN)

            def merge(i, blocks):
                n, dyn = T_MERGE, i * (4 * MERGE_TILES)
                oD_s, oF_s = (oD_hi, oD_lo), (oF_hi, oF_lo)
                for b in range(blocks):
                    y = bank[4 + 2 * (b % 2):6 + 2 * (b % 2)]
                    pe.wait_ge(merged, i * 4 + b + FREE - 1)
                    pe.wait_ge(o_lo, 8)
                    by_channel(pe, y[0][:, 0:T], n, dyn, oD_s, range(KD), True, False).then_inc(tile_used, 1)
                    by_channel(pe, y[0][:, 0:T], n + 1, dyn, oD_s, range(KD), False, True, KD).then_inc(tile_used, 1)
                    pe.wait_ge(o_lo, 12)
                    by_channel(pe, y[1][:, 0:T], n + 2, dyn, oF_s, range(KD), True, True).then_inc(tile_used, 1)
                    n += 3
                    if not isinstance(i, int) or 4 * i + b < KD - 2:
                        pe.wait_ge(gates_ready, i * 4 + b + 1)
                        for w in range(2):
                            by_channel(pe, bank[b % 2][:, w * T:(w + 1) * T], n + w, dyn, hT, range(KD), True, True)\
                                .then_inc(tile_used, 1)
                        n += 2

            with pe.Fori(0, KD // 4 - 1) as i:
                merge(i, 4)
            merge(KD // 4 - 1, 4)
            meet(pe, AFTER_MERGE)

            def rows_of(n, grow):
                for g in range(4):
                    for k in range(4):
                        cols = gcol[:, n, 4 * g + k:4 * g + k + 1].broadcast_to([P, P])
                        ins = mm(bank[4 + g][:, k * P:(k + 1) * P], cols, ident[:, :], start=True, stop=True)
                ins.then_inc(grow, 1)

            rows_of(0, grow_made)
            with pe.Fori(0, D // GROUP // 2) as i:
                for t in range(2 * OUT_TILES):
                    g, k = divmod(t, OUT_TILES)
                    pe.wait_ge(m_lo, k + 1)
                    if k == 0:
                        for tt in range(TT):
                            pe.wait_ge(y_taken[tt], i * 2 + g + FREE - 1)
                    by_token(pe, bank[2 * g:2 * g + 2], T_OUT + t, i * (2 * OUT_TILES), mT, 4 * k, 4, k == 0, k == OUT_TILES - 1)\
                        .then_inc(tile_used, 1)
            meet(pe, AFTER_OUT)
            pe.wait_ge(r_dve, 3 * TT)
            for g in range(8):
                for k in (2 * g, 2 * g + 1):
                    for t in range(TT):
                        at = (k % 2) * T + t * P
                        ins = tr(bank[g][:, at:at + P], ysb[:, t, k * P:(k + 1) * P], ident[:, :])
                ins.then_inc(h2_turned, 1)
            pe.wait_ge(h2_lo, 4)
            with pe.Fori(0, KF // 2) as i:
                for t in range(4):
                    b, w = divmod(t, 2)
                    if w == 0:
                        pe.wait_ge(gu_mixed, i * 2 + b + FREE - 1)
                    by_channel(pe, bank[2 * b + w][:, 0:T], T_FFN + t, i * 4, hT, range(KD), True, True)\
                        .then_inc(tile_used, 1)
            meet(pe, AFTER_FFN)
            rows_of(1, grow2_made)
            nd = len(DOWN_K)
            with pe.Fori(0, D // GROUP // 2) as i:
                for g in range(2):
                    for t, nk in enumerate(DOWN_K):
                        n = T_DOWN + g * nd + t
                        if t == 0:
                            for tt in range(TT):
                                pe.wait_ge(down_taken[tt], i * 2 + g + FREE - 1)
                        by_token(pe, bank[2 * g:2 * g + 2], n, i * (2 * nd), guT, sum(DOWN_K[:t]), nk, t == 0, t == nd - 1)\
                            .then_inc(tile_used, 1)
            meet(pe, AFTER_DOWN)

        @block.vector
        def _(dve):
            V = nc.vector
            dve.wait_ge(made, 6)
            V.memset(brow[0:1, 1, VH:GATES], 0.0).then_inc(small_v, 1)
            dve.wait_ge(x_squared, TT + 2)
            for t in range(TT):
                V.tensor_scalar(xs[:, t, :], xs[:, t, :], stat[:, 0, 1, t:t + 1], None, ALU.mult).then_inc(x_scaled, 1)
            dve.wait_ge(cond_ready, 2)
            for a in range(2 * KD):
                add_ada(dve, a, 0, a // KD)
                if a % KD == KD - 1:
                    g = a // KD
                    dve.wait_ge(ada_summed, g + 1)
                    V.tensor_tensor(adaT[:, g, :], bank[0][:, 0:KD], vecT[:, g * KD:(g + 1) * KD], ALU.add).then_inc(ada_biased, 1)
            dve.wait_ge(ada_biased, 2)
            V.scalar_tensor_tensor(mod[:, 0, :], adaT[:, 1, :], 1.0, gain[0], ALU.add, ALU.mult).then_inc(mod_ready, 1)
            dve.wait_ge(mod_ready, 1)
            dve.wait_ge(xT_ready, 8)
            for k in range(KD):
                V.tensor_scalar(hf[:, k, :], hf[:, k, :], mod[:, 0, k:k + 1], adaT[:, 0, k:k + 1], ALU.mult,
                                ALU.add).then_inc(h_ready, 1)
            split_lo(dve, T_FOX)
            for g in range(4):
                dve.wait_ge(h_hi, g + 1)
                V.tensor_tensor(hT[1][:, 4 * g:4 * g + 4, :], hf[:, 4 * g:4 * g + 4, :],
                                hT[0][:, 4 * g:4 * g + 4, :].bitcast(F32), ALU.subtract).then_inc(h_lo, 1)
            y, ny = small[:, 0, :, :], small[:, 4, :, :]
            dve.wait_ge(small_read, 2)
            V.tensor_tensor(small[:, 0, :, :], praw[:, :, VH:SMALL], bias_b[:, 0:1, :].broadcast_to([P, TT, GATES]),
                            ALU.add).then_inc(small_v, 1)
            dve.wait_ge(small_v, 2)
            V.tensor_scalar(small[:, 0, :, VH:GATES], small[:, 0, :, VH:GATES], -1.0, None, ALU.mult).then_inc(small_v, 1)
            dve.wait_ge(small_v, 3)
            V.tensor_scalar(ny, y, -1.0, None, ALU.mult).then_inc(small_v, 1)
            dve.wait_ge(small_v, 4)
            V.tensor_tensor(small[:, 1, :, :], y, ny, ALU.min).then_inc(small_v, 1)
            dve.wait_ge(small_v, 5)
            V.tensor_scalar(ny, y, 0.0, None, ALU.max).then_inc(small_v, 1)
            dve.wait_ge(small_v, 6)
            dve.wait_ge(small_s, 4)
            V.tensor_tensor(y, ny, small[:, 3, :, :], ALU.add).then_inc(small_v, 1)
            dve.wait_ge(small_v, 7)
            V.scalar_tensor_tensor(gd[:, :, 0:VH], y[:, :, 0:VH], -1.0, small[:, 5, 0:1, 0:VH].broadcast_to([P, TT, VH]),
                                   ALU.mult, ALU.mult).then_inc(decays_ready, 1)
            V.tensor_scalar(gd[:, :, VH:GATES], y[:, :, VH:GATES], -SQD, None, ALU.mult).then_inc(decays_ready, 1)
            dve.wait_ge(decays_ready, 2)

            dve.sem_inc(scores_masked, FREE)

            def fox_max(h):
                dve.wait_ge(scores_made, h + FREE + 1)
                dve.wait_ge(exp_made, h * 2 + FREE)
                V.tensor_tensor(fS[:, :, :], bank[4][:, 0:3 * P].rearrange("p (a b) -> p a b", a=3), CM[:, :, :],
                                ALU.add).then_inc(scores_masked, 1)
                dve.wait_ge(scores_masked, h + FREE + 1)
                V.tensor_reduce(fmax[:, 1:2], fS[:, 0:2, :].rearrange("p a b -> p (a b)"), AX.X, ALU.max).then_inc(max_made, 1)
                V.tensor_reduce(fmax[:, 0:1], fS[:, 2, :], AX.X, ALU.max).then_inc(max_made, 1)
                dve.wait_ge(max_made, h * 2 + 2)
                V.tensor_scalar(fneg[:, :], fmax[:, :], -SCALE, None, ALU.mult).then_inc(neg_made, 1)

            def fox_scale(h):
                dve.wait_ge(exp_made, h * 2 + 2 + FREE)
                V.reciprocal(finv[:, :], fsum[:, :]).then_inc(inv_made, 1)
                dve.wait_ge(inv_made, h + 1)
                V.tensor_scalar(fP[:, 0:2, :], fP[:, 0:2, :], finv[:, 1:2], None, ALU.mult).then_inc(probs_ready, 1)
                V.tensor_scalar(fP[:, 2, :], fP[:, 2, :], finv[:, 0:1], None, ALU.mult).then_inc(probs_ready, 1)

            def fox_turn(i, first):
                dyn, h = i * FOX_TILES, i * HEADS_A_TURN
                dve.wait_ge(fL_ready, i * (3 * HEADS_A_TURN) + FREE)
                V.tensor_copy(lfh[:, :, :], gd[:, :, bass.ds(i * HEADS_A_TURN + VH, HEADS_A_TURN)]).then_inc(lf_picked, 1)
                for t in range(FOX_TILES):
                    head = {1: None if first else h - 1, 7: h, 9: h + 1, 11: h + 2}.get(t)
                    if head is not None:
                        fox_max(head)
                    split_lo(dve, T_FOX + t + 1, dyn)
                    if head is not None:
                        fox_scale(head)

            fox_turn(0, True)
            with dve.Fori(1, TURNS) as i:
                fox_turn(i, False)
            fox_max(FH - 1)
            fox_scale(FH - 1)
            meet(dve, AFTER_FOX)

            def conv_taps(h, b, pr):
                for tap in range(1, CONV_K):
                    if tap == 1:
                        dve.wait_ge(conv_first, h * 4 + (b + 1))
                    else:
                        dve.wait_ge(conv_added, h * 8 + (2 * b + tap - 1))
                    V.scalar_tensor_tensor(cacc[:, b % 2, tap:T], bank[b % 2][:, 0:T - tap],
                                           cw[:, pr, b, CONV_K - 1 - tap:CONV_K - tap], cacc[:, b % 2, tap:T],
                                           ALU.mult, ALU.add).then_inc(conv_read if tap == CONV_K - 1 else conv_added, 1)

            def pick_gates(h):
                V.tensor_copy(gh[:, :, :], gd[:, :, bass.ds(h * 2, 2)]).then_inc(gates_picked, 1)
                V.tensor_copy(bh[:, :, :], beta[:, :, bass.ds(h * 2, 2)]).then_inc(gates_picked, 1)

            def output(h):
                dve.wait_ge(orn_ready, h + 1)
                dve.wait_ge(oD_ready, h + FREE)
                V.scalar_tensor_tensor(on[:, :, :].rearrange("p a b -> p (a b)"), bank[4][:, :], nwcol,
                                       rno[:, :, :].rearrange("p a b -> p (a b)"), ALU.mult, ALU.mult).then_inc(o_normed, 1)

            def bias_ada2(j):
                dve.wait_ge(ada2_summed, j + 1)
                V.tensor_tensor(ada_flat[:, bass.ds(j * 4 + 2 * KD, 4)], bank[7][:, 0:4],
                                vecT[:, bass.ds(j * 4 + 2 * KD, 4)], ALU.add).then_inc(ada2_biased, 1)

            ada_flat = adaT[:, :, :].rearrange("p a k -> p (a k)")

            def step(j, pr, n0, dyn, first=False, project=True, tiles=DN_TILES):
                for s in range(SLOTS):
                    for q in RUNS[s]:
                        if q < 4 * tiles:
                            split_lo(dve, n0 + q // 4 + 1, dyn, TILE, ((q % 4, q % 4 + 1),))
                    if s == 0:
                        if not first:
                            dve.wait_ge(vn_ready, j * 2)
                            dve.wait_ge(SLg_ready, j * 6)
                        pick_gates(j)
                    if s == 1:
                        if not first:
                            bias_ada2(j - 1)
                        dve.wait_ge(rn_ready, j + 1)
                        V.scalar_tensor_tensor(qk[:, pr, 0, :], qk[:, pr, 0, :], SCALE, rn[:, 0, :], ALU.mult,
                                               ALU.mult).then_inc(qkn_ready, 1)
                        V.tensor_tensor(qk[:, pr, 1, :], qk[:, pr, 1, :], rn[:, 1, :], ALU.mult).then_inc(qkn_ready, 1)
                    if s == 2 and not first:
                        output(j - 1)
                    if s == 3:
                        dve.wait_ge(dots_made, j + 1)
                        dve.wait_ge(E_ready, j + 1)
                        dve.wait_ge(gates_picked, j * 2 + 2)
                        if not first:
                            dve.wait_ge(LTm_ready, j * 6)
                        for u in range(4):
                            ch, v = divmod(u, 2)
                            V.scalar_tensor_tensor(LT[:, u, :], bank[2][:, ch * T + P:(ch + 1) * T], bh[:, ch, v:v + 1],
                                                   E[:, ch, v, :], ALU.mult, ALU.mult).then_inc(LT_ready, 1)
                        dve.wait_ge(LT_ready, j * 4 + 4)
                        if not first:
                            dve.wait_ge(vn_made, j)
                        V.tensor_tensor(Y[:, :, :], LT[:, :, :], LM[:, 0:1, :].broadcast_to([P, 4, P]),
                                        ALU.mult).then_inc(L1_ready, 1)
                        dve.wait_ge(L1_ready, j + 1)
                        V.tensor_tensor(XX[:, :, 1, :], ident[:, :].unsqueeze(1).broadcast_to([P, 4, P]), Y[:, :, :],
                                        ALU.subtract).then_inc(X_ready, 1)
                        dve.wait_ge(X_ready, j * 26 + 1)
                        V.transpose(XX[:, :, 0, :], XX[:, :, 1, :]).then_inc(X_ready, 1)
                    if s in (6, 8, 10, 12, 14, 16):
                        v = (s - 6) // 2
                        for u in range(4):
                            dve.wait_ge(XY_made, j * 24 + (4 * v + u + 1))
                            if v + 1 < TRANSPOSED:
                                V.tensor_tensor(XX[:, u, 0, :], XX[:, u, 0, :], bank[4 + u][:, P:2 * P],
                                                ALU.subtract).then_inc(X_ready, 1)
                                continue
                            if v < LEVELS - 2:
                                at, src = XX[:, u, :, :].rearrange("p a b -> p (a b)"), bank[4 + u][:, P:3 * P]
                            else:
                                at, src = XX[:, u, 1, :], bank[4 + u][:, 2 * P:3 * P]
                            V.tensor_tensor(at, at, src, ALU.subtract).then_inc(X_ready, 1)
                        if v + 1 < TRANSPOSED:
                            dve.wait_ge(X_ready, j * 26 + (2 + 4 * v + 4))
                            V.transpose(XX[:, :, 1, :], XX[:, :, 0, :]).then_inc(X_turned, 1)
                    if s == 19:
                        dve.wait_ge(R_made, j + 1)
                        V.tensor_tensor(rhs1[:, :, :], vtok[:, :, 1, :], bank[2][:, T:2 * T].rearrange("p (a b) -> p a b", a=2),
                                        ALU.subtract).then_inc(rhs_ready, 1)
                    for b in range(4):
                        if project and s == CONV_SLOTS[b]:
                            conv_taps(j + 1, b, 1 - pr)
                    if s in (8, 12):
                        ch = (s - 8) // 4
                        dve.wait_ge(Em_ready, j + 1)
                        if not first:
                            dve.wait_ge(o_made, j)
                        V.tensor_tensor(attn[:, ch, :, :], bank[2][:, ch * T:ch * T + P].unsqueeze(1).broadcast_to([P, 2, P]),
                                        Em[:, ch, :, :], ALU.mult).then_inc(attn_ready, 1)
                if not project:
                    output(j)
                    bias_ada2(j)

            for b in range(DN_TILES):
                split_lo(dve, T_DN + b + 1)
                if 1 <= b <= 4:
                    conv_taps(0, b - 1, 0)
            step(0, 0, T_DN + DN_TILES, 0, first=True)
            with dve.Fori(0, QKH // 2 - 1) as i:
                step(i * 2 + 1, 1, T_DN + 2 * DN_TILES, i * (2 * DN_TILES))
                step(i * 2 + 2, 0, T_DN + 3 * DN_TILES, i * (2 * DN_TILES))
            step(QKH - 1, 1, T_GATE, 0, project=False, tiles=GATE_TILES)
            meet(dve, AFTER_DN)

            dve.sem_inc(merged, FREE)
            V.scalar_tensor_tensor(mod[:, 1, :], adaT[:, 4, :], 1.0, gain[2], ALU.add, ALU.mult).then_inc(mod2_ready, 1)
            V.tensor_tensor(gcol[:, 0, :], adaT[:, 2, :], gain[1], ALU.mult).then_inc(mod2_ready, 1)
            V.tensor_tensor(gcol[:, 1, :], adaT[:, 5, :], gain[3], ALU.mult).then_inc(mod2_ready, 1)
            for g in range(12):
                src, lo, hi, k = (oD, oD_lo, oD_hi, 4 * g) if g < 8 else (oF, oF_lo, oF_hi, 4 * (g - 8))
                dve.wait_ge(o_hi, g + 1)
                V.tensor_tensor(lo[:, k:k + 4, :], src[:, k:k + 4, :], hi[:, k:k + 4, :].bitcast(F32),
                                ALU.subtract).then_inc(o_lo, 1)
            def merge(i, blocks):
                n, dyn = T_MERGE, i * (4 * MERGE_TILES)
                for b in range(blocks):
                    blk = i * 4 + b
                    tiles = MERGE_TILES if not isinstance(i, int) or blk < KD - 2 else 3
                    for t in range(tiles):
                        split_lo(dve, n + t + 1, dyn)
                        if t == 2:
                            used(dve, n + 2, dyn)
                            dve.wait_ge(gates_ready, blk + 1)
                            for w in range(2):
                                V.tensor_tensor(mt[:, w, :], gt[:, b % 2, w * T:(w + 1) * T],
                                                bank[4 + 2 * (b % 2) + w][:, 0:T], ALU.mult).then_inc(part_made, 1)
                            dve.wait_ge(part_made, blk * 2 + 2)
                            V.tensor_tensor(mF[:, bass.ds(blk, 1), :], mt[:, 0:1, :], mt[:, 1:2, :], ALU.add).then_inc(merged, 1)
                    n += tiles

            with dve.Fori(0, KD // 4 - 1) as i:
                merge(i, 4)
            merge(KD // 4 - 1, 4)
            meet(dve, AFTER_MERGE)
            for g in range(4):
                dve.wait_ge(m_hi, g + 1)
                V.tensor_tensor(mT[1][:, 4 * g:4 * g + 4, :], mF[:, 4 * g:4 * g + 4, :],
                                mT[0][:, 4 * g:4 * g + 4, :].bitcast(F32), ALU.subtract).then_inc(m_lo, 1)
            dve.sem_inc(y_taken[1], FREE)
            with dve.Fori(0, D // GROUP // 2) as i:
                dyn = i * (2 * OUT_TILES)
                for t in range(2 * OUT_TILES):
                    split_lo(dve, T_OUT + t + 1, dyn)
                    if t == OUT_TILES:
                        used(dve, T_OUT + OUT_TILES - 1, dyn)
                        V.tensor_copy(ysb[:, 1, bass.ds(i * (2 * GROUP), GROUP)], bank[1][:, :]).then_inc(y_taken[1], 1)
                used(dve, T_OUT + 2 * OUT_TILES - 1, dyn)
                V.tensor_copy(ysb[:, 1, bass.ds(i * (2 * GROUP) + GROUP, GROUP)], bank[3][:, :]).then_inc(y_taken[1], 1)
            meet(dve, AFTER_OUT)

            def residual(n, y, grow, done, act_done, landed):
                dve.wait_ge(act_done, TT + 2)
                for t in range(TT):
                    V.scalar_tensor_tensor(y[:, t, :], y[:, t, :], stat[:, n, 1, t:t + 1], grow, ALU.mult,
                                           ALU.mult).then_inc(done, 1)
                if landed is not None:
                    dve.wait_ge(landed, 16)
                for t in range(TT):
                    dve.wait_ge(done, t + 1)
                    V.tensor_tensor(x1[:, t, :], x1[:, t, :], y[:, t, :], ALU.add).then_inc(done, 1)

            residual(1, ysb, Grow[:, :], r_dve, r_act, x1_landed)
            dve.wait_ge(r_act, 2 * (TT + 2))
            dve.wait_ge(r_dve, 2 * TT)
            for t in range(TT):
                V.tensor_scalar(ysb[:, t, :], x1[:, t, :], stat[:, 2, 1, t:t + 1], None, ALU.mult).then_inc(r_dve, 1)
            for g in range(0, 8, 2):
                dve.wait_ge(h2_turned, g + 1)
                for k in (2 * g, 2 * g + 1):
                    V.tensor_scalar(h2f[:, k, :], bank[g][:, (k % 2) * T:(k % 2 + 1) * T], mod[:, 1, k:k + 1],
                                    adaT[:, 3, k:k + 1], ALU.mult, ALU.add).then_inc(h2_mod_dve, 1)
            for g in range(4):
                dve.wait_ge(h2_hi, g + 1)
                V.tensor_tensor(hT[1][:, 4 * g:4 * g + 4, :], h2f[:, 4 * g:4 * g + 4, :],
                                hT[0][:, 4 * g:4 * g + 4, :].bitcast(F32), ALU.subtract).then_inc(h2_lo, 1)
            dve.wait_ge(h2_lo, 4)
            dve.sem_inc(gu_mixed, FREE)
            with dve.Fori(0, KF // 2) as i:
                for t in range(4):
                    b, w = divmod(t, 2)
                    split_lo(dve, T_FFN + t + 1, i * 4)
                    if w == 1:
                        used(dve, T_FFN + t, i * 4)
                        dve.wait_ge(silu_made, i * 2 + (b + 1))
                        V.tensor_tensor(guf[:, b, :], sg[:, b, :], bank[2 * b + 1][:, 0:T], ALU.mult).then_inc(gu_mixed, 1)
                        dve.wait_ge(gu_hi, i * 2 + (b + 1))
                        V.tensor_tensor(guT[1][:, bass.ds(i * 2 + b, 1), :], guf[:, b:b + 1, :],
                                        guT[0][:, bass.ds(i * 2 + b, 1), :].bitcast(F32), ALU.subtract).then_inc(gu_lo, 1)
            meet(dve, AFTER_FFN)
            dve.sem_inc(down_taken[1], FREE)
            nd = len(DOWN_K)

            def down(i, more):
                for t in range(2 * nd):
                    if more or t < 2 * nd - 1:
                        split_lo(dve, T_DOWN + t + 1, i * (2 * nd), DOWN_K[(t + 1) % nd] * GROUP)
                    if t == nd:
                        used(dve, T_DOWN + nd - 1, i * (2 * nd))
                        V.tensor_copy(y2[:, 1, bass.ds(i * (2 * GROUP), GROUP)], bank[1][:, :]).then_inc(down_taken[1], 1)
                used(dve, T_DOWN + 2 * nd - 1, i * (2 * nd))
                V.tensor_copy(y2[:, 1, bass.ds(i * (2 * GROUP) + GROUP, GROUP)], bank[3][:, :]).then_inc(down_taken[1], 1)

            with dve.Fori(0, D // GROUP // 2 - 1) as i:
                down(i, True)
            down(D // GROUP // 2 - 1, False)
            meet(dve, AFTER_DOWN)
            residual(3, y2, Grow2[:, :], f_dve, f_act, None)


_INS = ["x", "c", "w_ada", "b_ada", "norm_gains", "w_in", "dn_conv", "dn_a_log", "dn_dt_bias", "dn_norm_w",
        "fox_f_bias", "w_branch_dn", "w_branch_fox", "w_out", "w_gate", "w_up", "w_down"]
_OUT = ((1, T, D), "float32")


def kernel(**inputs):
    import numpy as _np
    import concourse.bacc as _bacc
    from concourse import mybir as _mybir
    from concourse.bass_utils import run_bass_kernel_spmd as _run

    nc = _bacc.Bacc("TRN2", target_bir_lowering=False, num_devices=1, dynamic_dma_scratch_size=1024)
    arrays, args = {}, []
    for name in _INS:
        a = _np.ascontiguousarray(inputs[name])
        arrays[f"in_{name}_dram"] = a
        args.append(nc.dram_tensor(f"in_{name}_dram", a.shape, _mybir.dt.from_np(a.dtype), kind="ExternalInput").ap())
    shape, dtype = _OUT
    args.append(nc.dram_tensor("out_0_dram", shape, _mybir.dt.from_np(_np.dtype(dtype)), kind="ExternalOutput").ap())
    build(nc, *args)
    r = _run(nc, [arrays], core_ids=[0])
    return r.results[0]["out_0_dram"]
```

```python
from contextlib import ExitStack

import concourse.bass as bass
from concourse import mybir

F32 = mybir.dt.float32
F32R = mybir.dt.float32r
ALU = mybir.AluOpType
ACT = mybir.ActivationFunctionType
AX = mybir.AxisListType

P = 128
D = 2048
T = 256
KD = D // P
TT = T // P
QKH, VH, FH = 16, 32, 16
CONV_K = 4
QK_DIM, V_DIM = QKH * P, VH * P
CONV_DIM = 2 * QK_DIM + V_DIM
FOX = FH * P
FFN = 5632
KF = FFN // P
EPS = 1e-6
OFF_Z = CONV_DIM
OFF_B = OFF_Z + V_DIM
OFF_FOX = OFF_B + 2 * VH
OFF_F = OFF_FOX + 3 * FOX
OFF_M = OFF_F + FH
SMALL = 2 * VH + FH
GATES = VH + FH
TILE = 2048
GROUP = 512
GROUPS = D // GROUP
RAW, SPLIT, ADA = 4, 2, 4
HALVES = ((0, 2), (2, 4))
ADA_COLS = 4 * D // QKH
ADA_PIECES = 8

LEVELS = 7
SCALE = float(P) ** -0.5
SQD = float(P) ** 0.5
MASKED = -1e30
FREE = 2

HEADS_A_TURN = 4
FOX_TILES = 3 * HEADS_A_TURN
DN_TILES = 6
GATE_TILES = 4
MERGE_TILES = 5
OUT_TILES = 4
DOWN_K = [4, 4, 3] * 4
T_FOX = 0
T_DN = T_FOX + 3 * FH
T_GATE = T_DN + DN_TILES * QKH
T_MERGE = T_GATE + GATE_TILES
T_OUT = T_MERGE + MERGE_TILES * KD - GATE_TILES
T_FFN = T_OUT + OUT_TILES * (D // GROUP)
T_DOWN = T_FFN + 2 * KF
T_END = T_DOWN + len(DOWN_K) * (D // GROUP)
assert not any(n % RAW for n in (T_FOX, T_DN, T_GATE, T_MERGE, T_OUT, T_FFN, T_DOWN, T_END))

SLOTS = 24
QUARTERS = (2, 2, 1, 1, 2, 2, 0) + (1, 0) * 5 + (2, 1, 1, 1, 1, 1, 2)
GATE_QUARTERS = (1, 1, 1, 1, 1, 1, 0) + (1, 0) * 3 + (0, 0) * 2 + (1,) * 7


def runs(quarters):
    return [range(sum(quarters[:s]), sum(quarters[:s + 1])) for s in range(SLOTS)]


RUNS, GATE_RUNS = runs(QUARTERS), runs(GATE_QUARTERS)
END = [next(s for s in range(SLOTS) if 4 * b + 3 in RUNS[s]) for b in range(6)]
ADA_SLOTS = (3, 4, 5, 6, 8, 9, 10, 11, 13, 14, 15, 17, 18, 19, 20, 21)
ADA_SUMS = {2: (1, 2, 3), 3: (4, 5), 4: (6, 7), 5: (8, 9), 6: (10,)}
assert sum(QUARTERS) == 4 * DN_TILES and sum(GATE_QUARTERS) == 4 * GATE_TILES
CONV_SLOTS = (2, 7, 11, 18)
assert all(END[b] < CONV_SLOTS[b] for b in range(4))
TRANSPOSED = 5

AFTER_FOX, AFTER_DN, AFTER_MERGE, AFTER_OUT, AFTER_FFN, AFTER_DOWN = range(1, 7)


def build(nc, x, c, w_ada, b_ada, norm_gains, w_in, dn_conv, dn_a_log, dn_dt_bias, dn_norm_w,
          fox_f_bias, w_branch_dn, w_branch_fox, w_out, w_gate, w_up, w_down, out):
    def by_k(w):
        return w[0].rearrange("(k p) n -> p k n", p=P)

    ada_d, in_d, bdn_d, bfx_d, out_d, gate_d, up_d, down_d = map(
        by_k, (w_ada, w_in, w_branch_dn, w_branch_fox, w_out, w_gate, w_up, w_down))
    x_d = x[0].rearrange("(t p) d -> p t d", p=P)
    y_d = out[0].rearrange("(t p) d -> p t d", p=P)
    conv_d = dn_conv[0].rearrange("(b p) j -> p b j", p=P)

    ctx = ExitStack()
    with ctx:
        def sem(name):
            return ctx.enter_context(nc.semaphore(name))

        def sb(stack, name, shape, dt=F32):
            return stack.enter_context(nc.sbuf_tensor(name, shape, dt))

        raw = sb(ctx, "raw", [P, RAW, TILE])
        whi = sb(ctx, "whi", [P, SPLIT, TILE], F32R)
        wlo = sb(ctx, "wlo", [P, SPLIT, TILE], F32R)
        ones = sb(ctx, "ones", [P, P])
        ident = sb(ctx, "ident", [P, P])
        vecT = sb(ctx, "vecT", [P, 128 + 49])
        adaT = sb(ctx, "adaT", [P, 6, KD])
        mod = sb(ctx, "mod", [P, 2, KD])
        gcol = sb(ctx, "gcol", [P, 2, KD])
        eps = sb(ctx, "eps", [P, 1])
        diag = sb(ctx, "diag", [P, TT, P])
        condT = sb(ctx, "condT", [P, KD])
        stat = sb(ctx, "stat", [P, 4, 2, TT])
        part = sb(ctx, "part", [P, 2, TT, GROUPS])
        gain = {0: vecT[:, 96:112], 2: vecT[:, 112:128], 1: vecT[:, 144:160], 3: vecT[:, 160:176]}
        nwcol = vecT[:, 176:177]
        with ExitStack() as over_hT:
            hT = [sb(over_hT, "hT_hi", [P, KD, T], F32R), sb(over_hT, "hT_lo", [P, KD, T], F32R)]
            with ExitStack() as s:
                oD = sb(s, "oD", [P, VH, T])
                oF = sb(s, "oF", [P, FH, T])
                gd = sb(s, "gd", [P, TT, GATES])
                beta = sb(s, "beta", [P, TT, VH])
                U = sb(s, "U", [P, P])
                ONSL = sb(s, "ONSL", [P, 2, P])
                SL = ONSL[:, 1, :]
                with ExitStack() as a:
                    adar = sb(a, "adar", [P, ADA, TILE])
                    acc = sb(a, "acc", [P, 2, 2, GROUP])
                    wsm = sb(a, "wsm", [P, KD, SMALL])
                    small = sb(a, "small", [P, 6, TT, GATES])
                    praw = sb(a, "praw", [P, TT, SMALL])
                    rows = sb(a, "rows", [P, P])
                    rows2 = sb(a, "rows2", [P, P])
                    brow = sb(a, "brow", [1, 2, GATES])
                    bias_b = sb(a, "bias_b", [P, 2, GATES])
                    foxq = sb(a, "foxq", [P, 2, T])
                    foxk = sb(a, "foxk", [P, 2, T])
                    foxv = sb(a, "foxv", [P, TT, GROUP])
                    CM = sb(a, "CM", [P, 3, P])
                    fS = sb(a, "fS", [P, 3, P])
                    fP = sb(a, "fP", [P, 3, P])
                    fPT = sb(a, "fPT", [P, 3, P])
                    fL = sb(a, "fL", [P, 2, 3, P])
                    lfh = sb(a, "lfh", [P, TT, HEADS_A_TURN])
                    fmax = sb(a, "fmax", [P, 2])
                    fneg = sb(a, "fneg", [P, 2])
                    fsum = sb(a, "fsum", [P, 2])
                    finv = sb(a, "finv", [P, 2])
                with ExitStack() as a:
                    qk = sb(a, "qk", [P, 2, 2, T])
                    vc = sb(a, "vc", [P, 2, 2, T])
                    zc = sb(a, "zc", [P, 2, 2, T])
                    cacc = sb(a, "cacc", [P, 2, T])
                    cw = sb(a, "cw", [P, 2, 4, CONV_K])
                    gh = sb(a, "gh", [P, TT, 2])
                    bh = sb(a, "bh", [P, TT, 2])
                    on = sb(a, "on", [P, 2, T])
                    sq = sb(a, "sq", [P, 2, T])
                    rn = sb(a, "rn", [P, 2, T])
                    rno = sb(a, "rno", [P, 2, T])
                    SLg = sb(a, "SLg", [P, 2, 2, P])
                    gon = sb(a, "gon", [P, 2, P])
                    E = sb(a, "E", [P, 2, 2, P])
                    Em = sb(a, "Em", [P, 2, 2, P])
                    er = sb(a, "er", [P, 2, P])
                    ktok = sb(a, "ktok", [P, P])
                    vtok = sb(a, "vtok", [P, 2, 2, P])
                    qkg = sb(a, "qkg", [P, 2, 2, P])
                    kd = sb(a, "kd", [P, 2, P])
                    LT = sb(a, "LT", [P, 4, P])
                    LTm = sb(a, "LTm", [P, 2, 4, P])
                    attn = sb(a, "attn", [P, 2, 2, P])
                    XX = sb(a, "XX", [P, 4, 2, P])
                    Y = sb(a, "Y", [P, 4, P])
                    u0 = sb(a, "u0", [P, 2, P])
                    S1 = sb(a, "S1", [P, 2, P])
                    rhs1 = sb(a, "rhs1", [P, 2, P])
                    vn1 = sb(a, "vn1", [P, 2, P])
                    LM = sb(a, "LM", [P, LEVELS, P])
                    adar2 = sb(a, "adar2", [P, 2, 2, ADA_COLS])
                    acc2 = sb(a, "acc2", [P, ADA_COLS])
            with ExitStack() as s:
                oD_lo = sb(s, "oD_lo", [P, VH, T], F32R)
                oF_lo = sb(s, "oF_lo", [P, FH, T], F32R)
                oD_hi = sb(s, "oD_hi", [P, VH, T], F32R)
                oF_hi = sb(s, "oF_hi", [P, FH, T], F32R)
                mF = sb(s, "mF", [P, KD, T])
                gt = sb(s, "gt", [P, 2, 2 * T])
                mt = sb(s, "mt", [P, 2, T])
            with ExitStack() as s:
                mT = [sb(s, "mT_hi", [P, KD, T], F32R), sb(s, "mT_lo", [P, KD, T], F32R)]
                ysb = sb(s, "ysb", [P, TT, D])
                Grow = sb(s, "Grow", [P, D])
                assert T * (2 * KD) + TT * D + D <= 2 * KF * T
            with ExitStack() as s:
                h2f = sb(s, "h2f", [P, KD, T])
            with ExitStack() as s:
                guT = [sb(s, "guT_hi", [P, KF, T], F32R), sb(s, "guT_lo", [P, KF, T], F32R)]
                x1 = sb(s, "x1", [P, TT, D])
                sg = sb(s, "sg", [P, 2, T])
                guf = sb(s, "guf", [P, 2, T])
        with ExitStack() as s:
            y2 = sb(s, "y2", [P, TT, D])
            Grow2 = sb(s, "Grow2", [P, D])
        xs = oD[:, 0:KD, :].rearrange("p (t a) b -> p t (a b)", t=TT)
        hf = oD[:, KD:2 * KD, :]

        bank = [ctx.enter_context(nc.psum_tensor(f"bank{i}", [P, 512], F32)) for i in range(8)]

        raw_landed = [sem(f"raw_landed{i}") for i in range(RAW)]
        hi_done, lo_done, tile_used = sem("hi_done"), sem("lo_done"), sem("tile_used")
        ada_landed = [sem(f"ada_landed{i}") for i in range(ADA)]
        ada_used, ada_summed, ada_biased = sem("ada_used"), sem("ada_summed"), sem("ada_biased")
        ada2_landed = [sem("ada2_landed0"), sem("ada2_landed1")]
        ada2_scaled, ada2_used, ada2_summed, ada2_biased = map(sem, (
            "ada2_scaled", "ada2_used", "ada2_summed", "ada2_biased"))
        phase_over = sem("phase_over")
        rows_landed, x_landed, wsm_landed, brow_landed = map(sem, (
            "rows_landed", "x_landed", "wsm_landed", "brow_landed"))
        made, zeroed = sem("made"), sem("zeroed")
        rows_turned, cond_ready, x_squared, x_scaled, x_turned, xT_ready = map(sem, (
            "rows_turned", "cond_ready", "x_squared", "x_scaled", "x_turned", "xT_ready"))
        mod_ready, h_ready, h_hi, h_lo, small_summed, small_read = map(sem, (
            "mod_ready", "h_ready", "h_hi", "h_lo", "small_summed", "small_read"))
        small_v, small_s, decays_ready = sem("small_v"), sem("small_s"), sem("decays_ready")
        q_taken, k_taken, v_taken = map(sem, ("q_taken", "k_taken", "v_taken"))
        lf_picked, fL_ready, scores_made, scores_masked, max_made, neg_made, exp_made = map(sem, (
            "lf_picked", "fL_ready", "scores_made", "scores_masked", "max_made", "neg_made", "exp_made"))
        inv_made, probs_ready, probs_turned, probsT_ready, pv_made, pv_taken = map(sem, (
            "inv_made", "probs_ready", "probs_turned", "probsT_ready", "pv_made", "pv_taken"))
        conv_first, conv_added, conv_read, conv_done, z_read, gates_picked = map(sem, (
            "conv_first", "conv_added", "conv_read", "conv_done", "z_read", "gates_picked"))
        cw_landed = [sem("cw_landed0"), sem("cw_landed1")]
        sq_ready, norms_summed, norms_read, rn_ready, qkn_ready = map(sem, (
            "sq_ready", "norms_summed", "norms_read", "rn_ready", "qkn_ready"))
        SLg_ready, expo_made, E_ready, erow_made, er_ready, Em_ready, qkg_ready, kd_ready = map(sem, (
            "SLg_ready", "expo_made", "E_ready", "erow_made", "er_ready", "Em_ready", "qkg_ready", "kd_ready"))
        v_turned, vtok_ready, k_turned, ktok_ready, dots_made, LT_ready, attn_ready = map(sem, (
            "v_turned", "vtok_ready", "k_turned", "ktok_ready", "dots_made", "LT_ready", "attn_ready"))
        L1_ready, LTm_ready, X_turned, X_ready, Y_made, Y_ready, XY_made = map(sem, (
            "L1_ready", "LTm_ready", "X_turned", "X_ready", "Y_made", "Y_ready", "XY_made"))
        u0_made, u0_ready, S_made, S_ready, R_made, rhs_ready, vn_made, vn_ready, o_made = map(sem, (
            "u0_made", "u0_ready", "S_made", "S_ready", "R_made", "rhs_ready", "vn_made", "vn_ready", "o_made"))
        osq_ready, osum_made, osum_read, orn_ready, o_normed, oD_ready = map(sem, (
            "osq_ready", "osum_made", "osum_read", "orn_ready", "o_normed", "oD_ready"))
        mod2_ready, o_hi, o_lo, gates_ready, part_made, merged, m_hi, m_lo = map(sem, (
            "mod2_ready", "o_hi", "o_lo", "gates_ready", "part_made", "merged", "m_hi", "m_lo"))
        y_taken, y_squared = sem("y_taken"), sem("y_squared")
        grow_made, grow_taken = map(sem, ("grow_made", "grow_taken"))
        x1_landed, r_act, r_dve, h2_turned, h2_mod_act, h2_mod_dve, h2_hi, h2_lo = map(sem, (
            "x1_landed", "r_act", "r_dve", "h2_turned", "h2_mod_act", "h2_mod_dve", "h2_hi", "h2_lo"))
        silu_made, gu_mixed, gu_hi, gu_lo = map(sem, ("silu_made", "gu_mixed", "gu_hi", "gu_lo"))
        down_taken, down_squared = sem("down_taken"), sem("down_squared")
        grow2_made, grow2_taken, f_act, f_dve, stored = map(sem, (
            "grow2_made", "grow2_taken", "f_act", "f_dve", "stored"))

        block = ctx.enter_context(nc.Block())

        def load_tile(sp, n, src, dyn=0):
            k, cols = src.shape[1], src.shape[2]
            if n >= RAW:
                sp.wait_ge(lo_done, 4 * (n - RAW) + 4 + dyn * 4)
            sp.dma_start(raw[:, n % RAW, 0:k * cols].rearrange("p (k n) -> p k n", k=k), src)\
                .then_inc(raw_landed[n % RAW], 16)

        def split_hi(act, n, dyn=0, size=TILE, parts=HALVES):
            if parts[0][0] == 0:
                act.wait_ge(raw_landed[n % RAW], dyn * (16 // RAW) + 16 * (n // RAW + 1))
                if n >= SPLIT or not isinstance(dyn, int):
                    used(act, n - SPLIT, dyn)
            for a, b in parts:
                at = slice(a * TILE // 4, min(b * TILE // 4, size))
                nc.scalar.activation(whi[:, n % SPLIT, at], raw[:, n % RAW, at], ACT.Copy).then_inc(hi_done, b - a)

        def split_lo(dve, n, dyn=0, size=TILE, parts=HALVES):
            for a, b in parts:
                dve.wait_ge(hi_done, dyn * 4 + 4 * n + b)
                at = slice(a * TILE // 4, min(b * TILE // 4, size))
                nc.vector.tensor_tensor(wlo[:, n % SPLIT, at], raw[:, n % RAW, at],
                                        whi[:, n % SPLIT, at].bitcast(F32), ALU.subtract).then_inc(lo_done, b - a)

        def tile_ready(pe, n, dyn=0, quarters=4):
            pe.wait_ge(lo_done, dyn * 4 + 4 * n + quarters)

        def used(eng, n, dyn=0):
            eng.wait_ge(tile_used, dyn + n + 1)

        def by_channel(pe, dst, n, dyn, acts, ks, first, last, k0=0, split=None):
            hi, lo = acts
            step = min(8, len(ks))
            for k in ks:
                if k % step == 0:
                    tile_ready(pe, n, dyn, (k + step) // 4)
                if split and k % 4 == 0:
                    pe.wait_ge(split[0], max((k0 + k) // 4 + 1, split[1]))
                w_hi = whi[:, n % SPLIT, k * P:(k + 1) * P]
                w_lo = wlo[:, n % SPLIT, k * P:(k + 1) * P]
                nc.tensor.matmul(dst, w_hi, hi[:, k0 + k, :], start=first and k == ks[0], stop=False)
                nc.tensor.matmul(dst, w_hi, lo[:, k0 + k, :], start=False, stop=False)
                mm = nc.tensor.matmul(dst, w_lo, hi[:, k0 + k, :], start=False, stop=last and k == ks[-1])
            return mm

        def by_token(pe, dsts, n, dyn, acts, k0, nk, first, last):
            hi, lo = acts
            for k in range(nk):
                if k % 2 == 0:
                    tile_ready(pe, n, dyn, k + 2)
                w_hi = whi[:, n % SPLIT, k * GROUP:(k + 1) * GROUP]
                w_lo = wlo[:, n % SPLIT, k * GROUP:(k + 1) * GROUP]
                for t in range(TT):
                    at = slice(t * P, (t + 1) * P)
                    nc.tensor.matmul(dsts[t][:, :], hi[:, k0 + k, at], w_hi, start=first and k == 0, stop=False)
                    nc.tensor.matmul(dsts[t][:, :], hi[:, k0 + k, at], w_lo, start=False, stop=False)
                    mm = nc.tensor.matmul(dsts[t][:, :], lo[:, k0 + k, at], w_hi, start=False,
                                          stop=last and k == nk - 1)
            return mm

        def meet(eng, n):
            eng.drain().then_inc(phase_over, 1)
            eng.wait_ge(phase_over, 4 * n)

        def load_ada(sp, a):
            g, k4 = divmod(a, 4)
            if a >= ADA:
                sp.wait_ge(ada_used, 4 * (a - ADA) + 4)
            col = (g % 2) * D + (g // 2) * GROUP
            sp.dma_start(adar[:, a % ADA, :].rearrange("p (k n) -> p k n", k=4),
                         ada_d[:, 4 * k4:4 * k4 + 4, col:col + GROUP]).then_inc(ada_landed[a % ADA], 16)

        def add_ada(dve, a):
            g, k4 = divmod(a, 4)
            dve.wait_ge(ada_landed[a % ADA], 16 * (a // ADA + 1))
            for b in range(4):
                k, src = 4 * k4 + b, adar[:, a % ADA, b * GROUP:(b + 1) * GROUP]
                at = acc[:, g % 2, k % 2, :]
                if k < 2:
                    if k == 0 and g >= 2:
                        dve.wait_ge(ada_summed, g - 1)
                    ins = nc.vector.tensor_scalar(at, src, condT[:, k:k + 1], None, ALU.mult)
                else:
                    dve.wait_ge(ada_used, 4 * a + b - 1)
                    ins = nc.vector.scalar_tensor_tensor(at, src, condT[:, k:k + 1], at, ALU.mult, ALU.add)
                ins.then_inc(ada_used, 1)

        def sum_ada(pe, g):
            pe.wait_ge(ada_used, 16 * g + 16)
            if g >= 2:
                pe.wait_ge(ada_biased, g - 1)
            for k in range(4):
                for parity in range(2):
                    ins = nc.tensor.matmul(bank[5 + g % 2][:, k:k + 1], acc[:, g % 2, parity, k * P:(k + 1) * P],
                                           ones[:, 0:1], start=(parity == 0), stop=(parity == 1))
            ins.then_inc(ada_summed, 1)

        def load_ada2(sp, j, a):
            if not isinstance(j, int) or j > 0 or a >= 2:
                sp.wait_ge(ada2_used, j * (KD - 1) + {0: -2, 1: 0}.get(a, 2 * a - 3))
            sp.dma_start(adar2[:, a % 2, :, :], ada_d[:, 2 * a:2 * a + 2, bass.ds(j * ADA_COLS + 2 * D, ADA_COLS)])\
                .then_inc(ada2_landed[a % 2], 16)

        def scale_ada2(act, j, k, first):
            a, b = divmod(k, 2)
            if b == 0:
                act.wait_ge(ada2_landed[a % 2], j * (16 * ADA_PIECES // 2) + 16 * (a // 2 + 1))
            if k == 0 and not first:
                act.wait_ge(ada2_summed, j)
            at = adar2[:, a % 2, b, :]
            nc.scalar.activation(at if k else acc2[:, :], at, ACT.Copy, scale=condT[:, k:k + 1]).then_inc(ada2_scaled, 1)

        def sum_ada2(pool, j, k):
            a, b = divmod(k, 2)
            pool.wait_ge(ada2_scaled, j * KD + k + 1)
            if k > 1:
                pool.wait_ge(ada2_used, j * (KD - 1) + k - 1)
            nc.gpsimd.tensor_tensor(acc2[:, :], acc2[:, :], adar2[:, a % 2, b, :], ALU.add).then_inc(ada2_used, 1)

        TURNS = FH // HEADS_A_TURN

        def fox_src(i, t):
            if t < 4:
                return in_d[:, 4 * t:4 * t + 4, bass.ds(i * GROUP + (OFF_FOX + 2 * FOX), GROUP)]
            j, which = divmod(t - 4, 2)
            return in_d[:, :, bass.ds(i * GROUP + (OFF_FOX + which * FOX + j * P), P)]

        def dn_col(h, b):
            step, base = ((P, 0), (P, QK_DIM), (2 * P, 2 * QK_DIM), (2 * P, 2 * QK_DIM + P),
                          (2 * P, OFF_Z), (2 * P, OFF_Z + P))[b]
            return h * step + base

        @block.sync
        def _(sp):
            for dst, src in ((rows2[0:16, :], c[0].rearrange("(r n) -> r n", n=P)),
                             (rows2[16:32, :], norm_gains[0, 1].rearrange("(r n) -> r n", n=P)),
                             (rows2[32:48, :], norm_gains[0, 3].rearrange("(r n) -> r n", n=P)),
                             (rows2[48:49, :], dn_norm_w),
                             (rows[0:96, :], b_ada[0].rearrange("(r n) -> r n", n=P)),
                             (rows[96:112, :], norm_gains[0, 0].rearrange("(r n) -> r n", n=P)),
                             (rows[112:128, :], norm_gains[0, 2].rearrange("(r n) -> r n", n=P))):
                sp.dma_start(dst, src).then_inc(rows_landed, 16)
            for a in range(ADA):
                load_ada(sp, a)
            sp.dma_start(xs, x_d).then_inc(x_landed, 16)
            for a in range(ADA, 2 * KD):
                load_ada(sp, a)
                if a == 2 * ADA:
                    sp.dma_start(wsm[:, :, 0:2 * VH], in_d[:, :, OFF_B:OFF_FOX]).then_inc(wsm_landed, 16)
                    sp.dma_start(wsm[:, :, 2 * VH:SMALL], in_d[:, :, OFF_F:OFF_M]).then_inc(wsm_landed, 16)
                    sp.dma_start(brow[0:1, 0, 0:VH], dn_dt_bias).then_inc(brow_landed, 16)
                    sp.dma_start(brow[0:1, 0, VH:GATES], fox_f_bias).then_inc(brow_landed, 16)
                    sp.dma_start(brow[0:1, 1, 0:VH], dn_a_log).then_inc(brow_landed, 16)
                if a == 2 * KD - 2:
                    load_tile(sp, T_FOX, fox_src(0, 0))
            for n in range(1, RAW):
                load_tile(sp, T_FOX + n, fox_src(0, n))

            def fox_loads(i, loads):
                for n in range(RAW, RAW + loads):
                    src = fox_src(i, n) if n < FOX_TILES else fox_src(i + 1, n - FOX_TILES)
                    load_tile(sp, T_FOX + n, src, i * FOX_TILES)

            with sp.Fori(0, TURNS - 1) as i:
                fox_loads(i, FOX_TILES)
            fox_loads(TURNS - 1, FOX_TILES - RAW)

            def load_cw(h, pr):
                for b, (row, nb) in enumerate(((h, 1), (h + QKH, 1), (h * 2 + 2 * QKH, 2))):
                    sp.dma_start(cw[:, pr, b:b + nb, :], conv_d[:, bass.ds(row, nb), :]).then_inc(cw_landed[pr], 16)

            def dn_tile(n, h, b, dyn=0):
                load_tile(sp, n, in_d[:, :, bass.ds(dn_col(h, b), P)], dyn)

            def gate_src(blk, w):
                return in_d[:, :, bass.ds(blk * P + (OFF_M + w * D), P)]

            def dn_loads(j, pr, n0, dyn, more):
                if more:
                    sp.wait_ge(conv_read, j * 4 + 4)
                    load_cw(j + 2, pr)
                ada_pieces = {0: (), 1: (), 2: (2, 3), 3: (4, 5, 6), 4: (7, 8), 5: (9,)}
                for b in range(DN_TILES):
                    for a in ada_pieces[b]:
                        load_ada2(sp, j + a // ADA_PIECES, a % ADA_PIECES)
                    if b < DN_TILES - RAW:
                        dn_tile(n0 + RAW + b, j + 1, RAW + b, dyn)
                    elif more:
                        dn_tile(n0 + RAW + b, j + 2, b - (DN_TILES - RAW), dyn)
                    else:
                        load_tile(sp, n0 + RAW + b, gate_src(*divmod(b - (DN_TILES - RAW), 2)))

            for n in range(DN_TILES + RAW):
                if n == RAW:
                    sp.wait_ge(phase_over, 4 * AFTER_FOX)
                    load_cw(0, 0)
                    load_cw(1, 1)
                dn_tile(T_DN + n, n // DN_TILES, n % DN_TILES)
            load_ada2(sp, 0, 0)
            load_ada2(sp, 0, 1)
            dn_loads(0, 0, T_DN + DN_TILES, 0, True)
            with sp.Fori(0, QKH // 2 - 2) as i:
                dn_loads(i * 2 + 1, 1, T_DN + 2 * DN_TILES, i * (2 * DN_TILES), True)
                dn_loads(i * 2 + 2, 0, T_DN + 3 * DN_TILES, i * (2 * DN_TILES), True)
            dn_loads(QKH - 3, 1, T_DN + (QKH - 2) * DN_TILES, 0, True)
            dn_loads(QKH - 2, 0, T_DN + (QKH - 1) * DN_TILES, 0, False)
            def merge_src(i, m):
                sizes = [MERGE_TILES] * 4 if not isinstance(i, int) or i < KD // 4 - 1 else [MERGE_TILES] * 2 + [3] * 2
                b = 0
                while m >= sizes[b]:
                    m, b = m - sizes[b], b + 1
                if m >= 3:
                    return in_d[:, :, bass.ds(i * (4 * P) + (OFF_M + (m - 3) * D + (b + 2) * P), P)]
                w = (bdn_d[:, 0:KD, :], bdn_d[:, KD:2 * KD, :], bfx_d)[m]
                return w.rearrange("p k (b n) -> p k b n", n=P)[:, :, bass.ds(i * 4 + b, 1), :]\
                    .rearrange("p k b n -> p k (b n)")

            def merge_loads(i, loads):
                for m in range(RAW, RAW + loads):
                    src = merge_src(i, m) if m < 4 * MERGE_TILES else merge_src(i + 1, m - 4 * MERGE_TILES)
                    load_tile(sp, T_MERGE + m, src, i * (4 * MERGE_TILES))

            for m, pieces in ((0, (2,)), (1, (3,)), (2, (4, 5, 6, 7)), (3, ())):
                load_tile(sp, T_MERGE + m, merge_src(0, m))
                for a in pieces:
                    load_ada2(sp, QKH - 1, a)
            with sp.Fori(0, KD // 4 - 1) as i:
                merge_loads(i, 4 * MERGE_TILES)
            merge_loads(KD // 4 - 1, 4 * MERGE_TILES - GATE_TILES - RAW)
            with sp.Fori(0, D // GROUP // 2) as i:
                for t in range(2 * OUT_TILES):
                    g, k = divmod(t, OUT_TILES)
                    load_tile(sp, T_OUT + t, out_d[:, 4 * k:4 * k + 4, bass.ds(i * (2 * GROUP) + g * GROUP, GROUP)],
                              i * (2 * OUT_TILES))
            sp.wait_ge(m_lo, 4)
            sp.dma_start(x1[:, :, :], x_d).then_inc(x1_landed, 16)
            with sp.Fori(0, KF // 2) as i:
                for b in range(2):
                    for w, src in enumerate((gate_d, up_d)):
                        load_tile(sp, T_FFN + 2 * b + w, src[:, :, bass.ds(i * (2 * P) + b * P, P)], i * 4)
            with sp.Fori(0, D // GROUP // 2) as i:
                for g in range(2):
                    for t, nk in enumerate(DOWN_K):
                        k = sum(DOWN_K[:t])
                        load_tile(sp, T_DOWN + g * len(DOWN_K) + t,
                                  down_d[:, k:k + nk, bass.ds(i * (2 * GROUP) + g * GROUP, GROUP)],
                                  i * (2 * len(DOWN_K)))
            for t in range(TT):
                for half in range(2):
                    at = slice(half * D // 2, (half + 1) * D // 2)
                    sp.wait_ge(f_dve, 2 * t + half + 2)
                    sp.dma_start(y_d[:, t, at], x1[:, t, at]).then_inc(stored, 16)
            sp.wait_ge(stored, 16 * 2 * TT)

        @block.gpsimd
        def _(pool):
            G = nc.gpsimd
            G.memset(ones[:, :], 1.0).then_inc(made, 1)
            G.memset(eps[:, :], EPS).then_inc(made, 1)
            G.memset(ident[:, :], 0.0).then_inc(zeroed, 1)
            G.memset(U[:, :], 1.0).then_inc(zeroed, 1)
            G.memset(ONSL[:, :, :], 1.0).then_inc(zeroed, 1)
            G.memset(CM[:, :, :], 0.0).then_inc(zeroed, 1)
            pool.wait_ge(zeroed, 4)
            G.affine_select(out=ident[:, :], in_=ident[:, :], compare_op=ALU.not_equal, fill=1.0, base=0,
                            pattern=[[-1, P]], channel_multiplier=1).then_inc(made, 1)
            G.affine_select(out=U[:, :], in_=U[:, :], compare_op=ALU.is_ge, fill=0.0, base=0,
                            pattern=[[1, P]], channel_multiplier=-1).then_inc(made, 1)
            G.affine_select(out=SL, in_=SL, compare_op=ALU.is_gt, fill=0.0, base=0,
                            pattern=[[-1, P]], channel_multiplier=1).then_inc(made, 1)
            G.affine_select(out=CM[:, 1:3, :], in_=CM[:, 1:3, :], compare_op=ALU.is_ge, fill=MASKED, base=0,
                            pattern=[[0, 2], [-1, P]], channel_multiplier=1).then_inc(made, 1)
            pool.wait_ge(made, 6)
            pool.sem_inc(fL_ready, FREE)
            with pool.Fori(0, TURNS) as i:
                pool.wait_ge(lf_picked, i + 1)
                for j in range(HEADS_A_TURN):
                    pool.wait_ge(scores_made, i * HEADS_A_TURN + j + FREE - 1)
                    G.tensor_tensor(fL[:, j % 2, 0, :], U[:, :], lfh[:, 1, j:j + 1].broadcast_to([P, P]), ALU.mult).then_inc(fL_ready, 1)
                    G.tensor_tensor(fL[:, j % 2, 1, :], ones[:, :], lfh[:, 0, j:j + 1].broadcast_to([P, P]), ALU.mult).then_inc(fL_ready, 1)
                    G.tensor_tensor(fL[:, j % 2, 2, :], U[:, :], lfh[:, 0, j:j + 1].broadcast_to([P, P]), ALU.mult).then_inc(fL_ready, 1)
            meet(pool, AFTER_FOX)

            G.memset(LM[:, :, :], 0.0).then_inc(zeroed, 1)
            pool.wait_ge(zeroed, 5)

            def level(v):
                m = 1 << v
                return m, P // (2 * m), LM[:, v, :].rearrange("p (b h r) -> p b h r", h=2, r=m)[:, :, 1, :]

            for v in range(LEVELS):
                m, nb, at = level(v)
                G.memset(at, 1.0).then_inc(zeroed, 1)
            pool.wait_ge(zeroed, 5 + LEVELS)
            for v in range(LEVELS):
                m, nb, at = level(v)
                G.affine_select(out=at, in_=at, compare_op=ALU.is_ge, fill=0.0, base=0,
                                pattern=[[-2 * m, nb], [0, m]], channel_multiplier=1).then_inc(zeroed, 1)
            pool.wait_ge(zeroed, 5 + 2 * LEVELS)
            for v in range(LEVELS):
                m, nb, at = level(v)
                G.affine_select(out=at, in_=at, compare_op=ALU.is_ge, fill=0.0, base=m - 1,
                                pattern=[[2 * m, nb], [0, m]], channel_multiplier=-1).then_inc(made, 1)
            pool.wait_ge(made, 6 + LEVELS)

            def gate_output(h, pr):
                pool.wait_ge(o_normed, h + FREE + 1)
                G.tensor_tensor(oD[:, bass.ds(h * 2, 2), :], on[:, :, :], zc[:, pr, :, :], ALU.mult).then_inc(oD_ready, 1)

            pool.sem_inc(oD_ready, FREE)

            def delta(j, pr, first=False):
                pool.wait_ge(gates_picked, j * 2 + 2)
                if not first:
                    pool.wait_ge(erow_made, j)
                for v in range(2):
                    for ch in range(TT):
                        G.tensor_tensor(SLg[:, v, ch, :], SL, gh[:, ch, v:v + 1].broadcast_to([P, P]), ALU.mult).then_inc(SLg_ready, 1)
                for v in range(2):
                    G.tensor_tensor(gon[:, v, :], ones[:, :], gh[:, 1, v:v + 1].broadcast_to([P, P]), ALU.mult).then_inc(SLg_ready, 1)
                pool.wait_ge(E_ready, j + 1)
                if not first:
                    pool.wait_ge(attn_ready, j * 2)
                G.tensor_tensor(Em[:, :, :, :].rearrange("p a b n -> p (a b) n"),
                                E[:, :, :, :].rearrange("p a b n -> p (a b) n"),
                                U[:, :].unsqueeze(1).broadcast_to([P, 4, P]), ALU.mult).then_inc(Em_ready, 1)
                pool.wait_ge(qkn_ready, j * 2 + 2)
                pool.wait_ge(er_ready, j + 1)
                if not first:
                    pool.wait_ge(o_made, j)
                for v in range(2):
                    G.tensor_tensor(qkg[:, v, :, :], qk[:, pr, :, P:T],
                                    er[:, v, :].unsqueeze(1).broadcast_to([P, 2, P]), ALU.mult).then_inc(qkg_ready, 1)
                if not first:
                    gate_output(j - 1, 1 - pr)
                pool.wait_ge(LT_ready, j * 4 + 4)
                for v in range(1, LEVELS):
                    if v >= 3:
                        pool.wait_ge(Y_made, j * 24 + 4 * (v - 2))
                    elif not first:
                        pool.wait_ge(Y_made, j * 24)
                    G.tensor_tensor(LTm[:, v % 2, :, :], LT[:, :, :], LM[:, v:v + 1, :].broadcast_to([P, 4, P]),
                                    ALU.mult).then_inc(LTm_ready, 1)
                    for k in ADA_SUMS.get(v, ()):
                        sum_ada2(pool, j, k)
                pool.wait_ge(ktok_ready, j + 1)
                if not first:
                    pool.wait_ge(S_made, j)
                for v in range(2):
                    G.tensor_tensor(kd[:, v, :], ktok[:, :], E[:, 0, v, P - 1:P].broadcast_to([P, P]), ALU.mult).then_inc(kd_ready, 1)
                for k in range(max(ADA_SUMS[LEVELS - 1]) + 1, KD):
                    sum_ada2(pool, j, k)

            delta(0, 0, True)
            with pool.Fori(0, QKH // 2 - 1) as i:
                delta(i * 2 + 1, 1)
                delta(i * 2 + 2, 0)
            delta(QKH - 1, 1)
            gate_output(QKH - 1, 1)
            for n in (AFTER_DN, AFTER_MERGE, AFTER_OUT, AFTER_FFN, AFTER_DOWN):
                meet(pool, n)

        @block.scalar
        def _(act):
            A = nc.scalar.activation

            def ln_exp():
                act.preload_act_table_set("natural_log_exp_and_others")

            def silu():
                act.preload_act_table(ACT.Silu)

            def rms(n, src, scratch, done, base):
                total, inverse = stat[:, n, 0, :], stat[:, n, 1, :]
                for t in range(TT):
                    A(scratch, src[:, t, :], ACT.Square, accum_out=total[:, t:t + 1]).then_inc(done, 1)
                    act.wait_ge(done, base + t + 1)
                A(inverse, total, ACT.Ln, bias=eps[:, 0:1], scale=1.0 / D).then_inc(done, 1)
                act.wait_ge(done, base + TT + 1)
                A(inverse, inverse, ACT.Exp, scale=-0.5).then_inc(done, 1)

            silu()
            act.wait_ge(made, 6)
            act.wait_ge(rows_turned, 1)
            A(vecT[:, :], bank[0][:, 0:177], ACT.Copy).then_inc(cond_ready, 1)
            A(condT[:, :], bank[0][:, 128:144], ACT.Silu).then_inc(cond_ready, 1)
            ln_exp()
            act.wait_ge(x_landed, 16)
            rms(0, xs, hf.rearrange("p a b -> p (a b)")[:, 0:D], x_squared, 0)
            for g in range(8):
                act.wait_ge(x_turned, g + 1)
                A(hf[:, 2 * g:2 * g + 2, :], bank[1 + g % 4][:, :].rearrange("p (a b) -> p a b", a=2),
                  ACT.Copy).then_inc(xT_ready, 1)
            act.wait_ge(xT_ready, 8)
            for g in range(4):
                act.wait_ge(mod_ready, g + 1)
                for k in range(4 * g, 4 * g + 4):
                    A(hf[:, k, :], hf[:, k, :], ACT.Identity, bias=adaT[:, 0, k:k + 1],
                      scale=mod[:, 0, k:k + 1]).then_inc(h_ready, 1)
                act.wait_ge(h_ready, 4 * g + 4)
                A(hT[0][:, 4 * g:4 * g + 4, :], hf[:, 4 * g:4 * g + 4, :], ACT.Copy).then_inc(h_hi, 1)
                if g == 2:
                    split_hi(act, T_FOX)

            def log_decays():
                act.preload_act_table(ACT.Sigmoid)
                act.wait_ge(small_summed, 1)
                A(praw[:, :, :].rearrange("p t n -> p (t n)"), bank[7][:, 0:TT * SMALL], ACT.Copy).then_inc(small_read, 1)
                A(bias_b[:, :, :].rearrange("p t n -> p (t n)"), bank[7][:, 256:256 + 2 * GATES], ACT.Copy).then_inc(small_read, 1)
                act.wait_ge(small_read, 2)
                A(beta[:, :, :], praw[:, :, 0:VH], ACT.Sigmoid).then_inc(small_s, 1)
                ln_exp()
                A(small[:, 5, 0, 0:VH], bias_b[:, 1, 0:VH], ACT.Exp).then_inc(small_s, 1)
                act.wait_ge(small_v, 6)
                A(small[:, 2, :, :], small[:, 1, :, :], ACT.Exp).then_inc(small_s, 1)
                act.wait_ge(small_s, 3)
                A(small[:, 3, :, :], small[:, 2, :, :], ACT.Ln, bias=ones[:, 0:1]).then_inc(small_s, 1)

            for s in (q_taken, k_taken, v_taken, exp_made, probsT_ready, pv_taken):
                act.sem_inc(s, FREE)

            def fox_take(h, j, which, n, dyn):
                taken, dst = ((q_taken, foxq), (k_taken, foxk))[which]
                used(act, n, dyn)
                act.wait_ge(scores_made, h + FREE - 1)
                A(dst[:, j % 2, :], bank[2 + which][:, 0:T], ACT.Copy).then_inc(taken, 1)

            def fox_exps(h):
                act.wait_ge(neg_made, h + 1)
                act.wait_ge(probs_turned, h + FREE)
                A(fP[:, 0:2, :], fS[:, 0:2, :], ACT.Exp, bias=fneg[:, 1:2], scale=SCALE,
                  accum_out=fsum[:, 1:2]).then_inc(exp_made, 1)
                A(fP[:, 2, :], fS[:, 2, :], ACT.Exp, bias=fneg[:, 0:1], scale=SCALE,
                  accum_out=fsum[:, 0:1]).then_inc(exp_made, 1)

            def fox_probsT(h):
                act.wait_ge(probs_turned, h + FREE + 1)
                act.wait_ge(pv_made, h + FREE)
                A(fPT[:, :, :].rearrange("p a b -> p (a b)"), bank[5][:, 0:3 * P], ACT.Copy).then_inc(probsT_ready, 1)

            def fox_o(h):
                act.wait_ge(pv_made, h + FREE + 1)
                A(oF[:, bass.ds(h, 1), :], bank[6][:, 0:T].unsqueeze(1), ACT.Copy).then_inc(pv_taken, 1)

            def fox_turn(i, first):
                dyn, h = i * FOX_TILES, i * HEADS_A_TURN
                for t in range(FOX_TILES):
                    split_hi(act, T_FOX + t + 1, dyn)
                    if t == 1 and first:
                        log_decays()
                    if t == 0 and not first:
                        fox_take(h - 1, HEADS_A_TURN - 1, 1, T_FOX - 1, dyn)
                        fox_probsT(h - 2)
                    if t == 1 and not first:
                        fox_o(h - 2)
                        fox_exps(h - 1)
                    if t == 2 and not first:
                        fox_probsT(h - 1)
                    if t == 3 and not first:
                        fox_o(h - 1)
                    if t == 4:
                        used(act, T_FOX + 3, dyn)
                        act.wait_ge(pv_made, h + FREE)
                        for tt in range(TT):
                            A(foxv[:, tt, :], bank[tt][:, :], ACT.Copy).then_inc(v_taken, 1)
                    if t >= 5:
                        j, which = divmod(t - 5, 2)
                        fox_take(h + j, j, which, T_FOX + t - 1, dyn)
                    if t in (7, 9, 11):
                        fox_exps(h + (t - 7) // 2)
                    if t in (8, 10):
                        fox_probsT(h + (t - 8) // 2)
                    if t in (9, 11):
                        fox_o(h + (t - 9) // 2)

            fox_turn(0, True)
            with act.Fori(1, TURNS) as i:
                fox_turn(i, False)
            fox_take(FH - 1, HEADS_A_TURN - 1, 1, T_DN - 1, 0)
            fox_probsT(FH - 2)
            fox_o(FH - 2)
            fox_exps(FH - 1)
            fox_probsT(FH - 1)
            fox_o(FH - 1)
            meet(act, AFTER_FOX)

            def conv_tap(h, b, pr, h2):
                used(act, T_DN + b, h * DN_TILES)
                if b == 0:
                    act.wait_ge(cw_landed[pr], h2 * 48 + 48)
                if b >= 2 or not (isinstance(h, int) and h == 0):
                    act.wait_ge(conv_done, h * 4 + (b - 1))
                A(cacc[:, b % 2, :], bank[b % 2][:, 0:T], ACT.Copy, scale=cw[:, pr, b, 3:4]).then_inc(conv_first, 1)

            def conv_silu(h, b, pr):
                act.wait_ge(conv_read, h * 4 + (b + 1))
                A(qk[:, pr, b, :] if b < 2 else vc[:, pr, b - 2, :], cacc[:, b % 2, :], ACT.Silu).then_inc(conv_done, 1)

            act.sem_inc(o_normed, FREE)

            def z_silu(h, b, pr):
                used(act, T_DN + 4 + b, h * DN_TILES)
                if not isinstance(h, int) or h >= 2:
                    act.wait_ge(oD_ready, h + FREE - 1)
                A(zc[:, pr, b, :], bank[b][:, 0:T], ACT.Silu).then_inc(z_read, 1)

            def step(j, pr, j2, n0, dyn, first=False, project=True):
                for s in range(SLOTS):
                    for q in (RUNS if project else GATE_RUNS)[s]:
                        split_hi(act, n0 + q // 4 + 1, dyn, TILE, ((q % 4, q % 4 + 1),))
                    if s in ADA_SLOTS:
                        scale_ada2(act, j, ADA_SLOTS.index(s), first)
                    if s == 4:
                        silu()
                    for b in range(4):
                        if project and s == CONV_SLOTS[b]:
                            conv_tap(j + 1, b, 1 - pr, j2)
                        if project and s == CONV_SLOTS[b] + 2:
                            conv_silu(j + 1, b, 1 - pr)
                    if s == 0:
                        z_silu(j, 1, pr)
                        act.wait_ge(conv_done, j * 4 + 2)
                        if not first:
                            act.wait_ge(osum_made, j)
                        A(sq[:, :, :], qk[:, pr, :, :], ACT.Square).then_inc(sq_ready, 1)
                    if s == 1:
                        ln_exp()
                        if not first:
                            act.wait_ge(o_normed, j + FREE - 1)
                            act.wait_ge(osum_made, j)
                            A(rno[:, :, :].rearrange("p a b -> p (a b)"), bank[5][:, :], ACT.Ln, bias=eps[:, 0:1],
                              scale=1.0 / P).then_inc(osum_read, 1)
                        act.wait_ge(norms_summed, j + 1)
                        A(rn[:, :, :].rearrange("p a b -> p (a b)"), bank[2][:, :], ACT.Ln, bias=eps[:, 0:1]).then_inc(norms_read, 1)
                        if not first:
                            act.wait_ge(osum_read, j)
                            A(rno[:, :, :], rno[:, :, :], ACT.Exp, scale=-0.5).then_inc(orn_ready, 1)
                        act.wait_ge(norms_read, j + 1)
                        A(rn[:, :, :], rn[:, :, :], ACT.Exp, scale=-0.5).then_inc(rn_ready, 1)
                        act.wait_ge(expo_made, j + 1)
                        if not first:
                            act.wait_ge(kd_ready, j * 2)
                            act.wait_ge(LT_ready, j * 4)
                        A(E[:, :, :, :].rearrange("p a b n -> p (a b n)"), bank[3][:, :], ACT.Exp).then_inc(E_ready, 1)
                        act.wait_ge(erow_made, j + 1)
                        A(er[:, :, :].rearrange("p a b -> p (a b)"), bank[6][:, 0:T], ACT.Exp).then_inc(er_ready, 1)
                    if s == 2:
                        act.wait_ge(v_turned, j + 1)
                        if not first:
                            act.wait_ge(rhs_ready, j)
                        A(vtok[:, :, :, :].rearrange("p a b n -> p (a b n)"), bank[7][:, :], ACT.Copy).then_inc(vtok_ready, 1)
                    if s == 3:
                        act.wait_ge(k_turned, j + 1)
                        A(ktok[:, :], bank[5][:, 0:P], ACT.Copy).then_inc(ktok_ready, 1)
                    if s in (5, 7, 9, 11, 13, 15):
                        for u in range(4):
                            act.wait_ge(Y_made, j * 24 + (4 * ((s - 5) // 2) + u + 1))
                            A(Y[:, u, :], bank[4 + u][:, 0:P], ACT.Copy).then_inc(Y_ready, 1)
                    if s == 17:
                        act.wait_ge(u0_made, j + 1)
                        for v in range(2):
                            A(u0[:, v, :], bank[2][:, v * P:(v + 1) * P], ACT.Copy, scale=bh[:, 0, v:v + 1]).then_inc(u0_ready, 1)
                    if s == 18:
                        act.wait_ge(S_made, j + 1)
                        A(S1[:, :, :].rearrange("p a b -> p (a b)"), bank[3][:, 0:T], ACT.Copy).then_inc(S_ready, 1)
                    if s == 20:
                        act.wait_ge(vn_made, j + 1)
                        for v in range(2):
                            A(vn1[:, v, :], bank[3][:, T + v * P:T + (v + 1) * P], ACT.Copy,
                              scale=bh[:, 1, v:v + 1]).then_inc(vn_ready, 1)
                    if s == 21:
                        act.wait_ge(o_made, j + 1)
                        A(sq[:, :, :].rearrange("p a b -> p (a b)"), bank[4][:, :], ACT.Square).then_inc(osq_ready, 1)
                    if s == END[4] + 1 and project:
                        z_silu(j + 1, 0, 1 - pr)
                    if s == 22 and not project:
                        ln_exp()
                        act.wait_ge(o_normed, j + FREE)
                        act.wait_ge(osum_made, j + 1)
                        A(rno[:, :, :].rearrange("p a b -> p (a b)"), bank[5][:, :], ACT.Ln, bias=eps[:, 0:1],
                          scale=1.0 / P).then_inc(osum_read, 1)
                        act.wait_ge(osum_read, j + 1)
                        A(rno[:, :, :], rno[:, :, :], ACT.Exp, scale=-0.5).then_inc(orn_ready, 1)

            silu()
            for b in range(DN_TILES):
                split_hi(act, T_DN + b + 1)
                if 1 <= b <= 4:
                    conv_tap(0, b - 1, 0, 0)
                    conv_silu(0, b - 1, 0)
                if b == 5:
                    z_silu(0, 0, 0)
            step(0, 0, 0, T_DN + DN_TILES, 0, first=True)
            with act.Fori(0, QKH // 2 - 1) as i:
                step(i * 2 + 1, 1, i + 1, T_DN + 2 * DN_TILES, i * (2 * DN_TILES))
                step(i * 2 + 2, 0, i + 1, T_DN + 3 * DN_TILES, i * (2 * DN_TILES))
            step(QKH - 1, 1, 0, T_GATE, 0, project=False)
            meet(act, AFTER_DN)

            def high_outputs(part):
                for g in range(4 * part, 4 * part + 4):
                    src, dst, k = (oD, oD_hi, 4 * g) if g < 8 else (oF, oF_hi, 4 * (g - 8))
                    A(dst[:, k:k + 4, :], src[:, k:k + 4, :], ACT.Copy).then_inc(o_hi, 1)

            def first_gates():
                used(act, T_GATE + GATE_TILES - 1)
                for b in range(2):
                    A(gt[:, b, :], bank[b][:, :], ACT.Sigmoid).then_inc(gates_ready, 1)

            act.preload_act_table(ACT.Sigmoid)

            def merge(i, blocks):
                n, dyn = T_MERGE, i * (4 * MERGE_TILES)
                for b in range(blocks):
                    gates = not isinstance(i, int) or 4 * i + b < KD - 2
                    for t in range(MERGE_TILES if gates else 3):
                        if isinstance(i, int) and 4 * i + b == 0 and t < 3:
                            high_outputs(t)
                            if t == 1:
                                first_gates()
                        split_hi(act, n + t + 1, dyn)
                    if gates:
                        used(act, n + MERGE_TILES - 1, dyn)
                        act.wait_ge(merged, i * 4 + b + FREE + 1)
                        A(gt[:, b % 2, :], bank[b % 2][:, :], ACT.Sigmoid).then_inc(gates_ready, 1)
                    n += MERGE_TILES if gates else 3

            merge(0, 4)
            with act.Fori(1, KD // 4 - 1) as i:
                merge(i, 4)
            merge(KD // 4 - 1, 4)
            meet(act, AFTER_MERGE)
            for g in range(4):
                A(mT[0][:, 4 * g:4 * g + 4, :], mF[:, 4 * g:4 * g + 4, :], ACT.Copy).then_inc(m_hi, 1)

            def squares(n, g, last, done):
                used(act, last)
                for t in range(TT):
                    A((ysb, y2)[n][:, t, g * GROUP:(g + 1) * GROUP], bank[2 * (g % 2) + t][:, :], ACT.Square,
                      accum_out=part[:, n, t, g:g + 1]).then_inc(done, 1)

            def inverse_rms(n, done, at):
                A(stat[:, n, 1, :], stat[:, n, 0, :], ACT.Ln, bias=eps[:, 0:1], scale=1.0 / D).then_inc(done, 1)
                act.wait_ge(done, at + 1)
                A(stat[:, n, 1, :], stat[:, n, 1, :], ACT.Exp, scale=-0.5).then_inc(done, 1)

            for g in range(4):
                act.wait_ge(grow_made, 1)
                A(Grow[:, g * GROUP:(g + 1) * GROUP], bank[4 + g][:, :], ACT.Copy).then_inc(grow_taken, 1)
            ln_exp()
            for t in range(GROUPS * OUT_TILES):
                split_hi(act, T_OUT + t + 1)
                if t % OUT_TILES == 0 and t:
                    squares(0, t // OUT_TILES - 1, T_OUT + t - 1, y_squared)
            squares(0, GROUPS - 1, T_FFN - 1, y_squared)
            meet(act, AFTER_OUT)
            act.wait_ge(r_dve, 1)
            inverse_rms(1, r_act, 0)
            split_hi(act, T_FFN + 1)
            for t in range(TT):
                act.wait_ge(r_dve, t + 2)
                A(ysb[:, t, :], x1[:, t, :], ACT.Square, accum_out=stat[:, 2, 0, t:t + 1]).then_inc(r_act, 1)
            act.wait_ge(r_act, 2 + TT)
            inverse_rms(2, r_act, 2 + TT)
            for m in range(4):
                g = 2 * m + 1
                act.wait_ge(h2_turned, g + 1)
                for k in (2 * g, 2 * g + 1):
                    A(h2f[:, k, :], bank[g][:, (k % 2) * T:(k % 2 + 1) * T], ACT.Identity,
                      bias=adaT[:, 3, k:k + 1], scale=mod[:, 1, k:k + 1]).then_inc(h2_mod_act, 1)
                act.wait_ge(h2_mod_act, 2 * m + 2)
                act.wait_ge(h2_mod_dve, 2 * m + 2)
                A(hT[0][:, 4 * m:4 * m + 4, :], h2f[:, 4 * m:4 * m + 4, :], ACT.Copy).then_inc(h2_hi, 1)
            act.wait_ge(h2_lo, 4)
            silu()
            def ffn(i):
                dyn = i * 4
                for t in range(4):
                    b, w = divmod(t, 2)
                    if t or not isinstance(i, int):
                        split_hi(act, T_FFN + t + 1, dyn)
                    if w == 1:
                        used(act, T_FFN + 2 * b, dyn)
                        act.wait_ge(gu_mixed, i * 2 + b + FREE - 1)
                        A(sg[:, b, :], bank[2 * b][:, 0:T], ACT.Silu).then_inc(silu_made, 1)
                        act.wait_ge(gu_mixed, i * 2 + b + FREE + 1)
                        A(guT[0][:, bass.ds(i * 2 + b, 1), :], guf[:, b:b + 1, :], ACT.Copy).then_inc(gu_hi, 1)

            ffn(0)
            with act.Fori(1, KF // 2) as i:
                ffn(i)
            meet(act, AFTER_FFN)
            for g in range(4):
                act.wait_ge(grow2_made, 1)
                A(Grow2[:, g * GROUP:(g + 1) * GROUP], bank[4 + g][:, :], ACT.Copy).then_inc(grow2_taken, 1)
            ln_exp()
            nd = len(DOWN_K)
            for t in range(GROUPS * nd):
                if t < GROUPS * nd - 1:
                    split_hi(act, T_DOWN + t + 1, 0, DOWN_K[(t + 1) % nd] * GROUP)
                if t % nd == 0 and t:
                    squares(1, t // nd - 1, T_DOWN + t - 1, down_squared)
            squares(1, GROUPS - 1, T_END - 1, down_squared)
            meet(act, AFTER_DOWN)
            act.wait_ge(f_dve, 1)
            inverse_rms(3, f_act, 0)

        @block.tensor
        def _(pe):
            mm = nc.tensor.matmul
            tr = nc.tensor.transpose
            for s in (scores_made, pv_made, probs_turned):
                pe.sem_inc(s, FREE)
            pe.wait_ge(made, 6)
            pe.wait_ge(rows_landed, 7 * 16)
            tr(bank[0][:, 0:P], rows[:, :], ident[:, :])
            tr(bank[0][:, P:P + 49], rows2[0:49, :], ident[0:49, 0:49]).then_inc(rows_turned, 1)
            sum_ada(pe, 0)
            pe.wait_ge(x_landed, 16)
            pe.wait_ge(x_scaled, TT)
            for g in range(8):
                if g >= 4:
                    pe.wait_ge(xT_ready, g - 3)
                for k in (2 * g, 2 * g + 1):
                    for t in range(TT):
                        at = (k % 2) * T + t * P
                        ins = mm(bank[1 + g % 4][:, at:at + P], xs[:, t, k * P:(k + 1) * P], diag[:, t, :],
                                 start=True, stop=True)
                ins.then_inc(x_turned, 1)
            for g in range(1, 8):
                sum_ada(pe, g)
            pe.wait_ge(xT_ready, 8)

            def small_products():
                pe.wait_ge(wsm_landed, 32)
                pe.wait_ge(h_ready, KD)
                for t in range(TT):
                    for k in range(KD):
                        mm(bank[7][:, t * SMALL:(t + 1) * SMALL], hf[:, k, t * P:(t + 1) * P], wsm[:, k, :],
                           start=(k == 0), stop=(k == KD - 1))
                pe.wait_ge(brow_landed, 48)
                pe.wait_ge(small_v, 1)
                mm(bank[7][:, 256:256 + 2 * GATES], ones[0:1, :], brow[0:1, :, :].rearrange("p a b -> p (a b)"),
                   start=True, stop=True).then_inc(small_summed, 1)

            def fox_scores(h, j):
                s = bank[4]
                pe.wait_ge(q_taken, h + FREE + 1)
                pe.wait_ge(k_taken, h + FREE + 1)
                pe.wait_ge(fL_ready, h * 3 + 3 + FREE)
                pe.wait_ge(scores_masked, h + FREE)
                mm(s[:, 0:T], foxq[:, j % 2, P:T], foxk[:, j % 2, :], start=True, stop=False)
                mm(s[:, 0:P], fL[:, j % 2, 1, :], SL, start=False, stop=False)
                mm(s[:, 0:T], fL[:, j % 2, 0, :], ONSL[:, :, :].rearrange("p a b -> p (a b)"), start=False, stop=True)
                mm(s[:, T:T + P], foxq[:, j % 2, 0:P], foxk[:, j % 2, 0:P], start=True, stop=False)
                mm(s[:, T:T + P], fL[:, j % 2, 2, :], SL, start=False, stop=True).then_inc(scores_made, 1)

            def fox_turn(h):
                pe.wait_ge(probs_ready, h * 2 + 2)
                pe.wait_ge(probsT_ready, h + FREE)
                for n, blk in enumerate((2, 0, 1)):
                    ins = tr(bank[5][:, n * P:(n + 1) * P], fP[:, blk, :], ident[:, :])
                ins.then_inc(probs_turned, 1)

            def fox_pv(h, j):
                pe.wait_ge(probsT_ready, h + FREE + 1)
                pe.wait_ge(pv_taken, h + FREE)
                v = foxv[:, :, j * P:(j + 1) * P]
                mm(bank[6][:, 0:P], v[:, 0, :], fPT[:, 0, :], start=True, stop=True)
                mm(bank[6][:, P:T], v[:, 0, :], fPT[:, 1, :], start=True, stop=False)
                mm(bank[6][:, P:T], v[:, 1, :], fPT[:, 2, :], start=False, stop=True).then_inc(pv_made, 1)

            def fox(i, first):
                dyn, h = i * FOX_TILES, i * HEADS_A_TURN
                for t in range(FOX_TILES):
                    n = T_FOX + t
                    if t < 4:
                        if t == 0:
                            pe.wait_ge(v_taken, i * TT + FREE)
                        if first:
                            pe.wait_ge(h_lo, t + 1)
                        ins = by_token(pe, bank[0:2], n, dyn, hT, 4 * t, 4, t == 0, t == 3)
                    else:
                        j, which = divmod(t - 4, 2)
                        pe.wait_ge((q_taken, k_taken)[which], h + j + FREE)
                        ins = by_channel(pe, bank[2 + which][:, 0:T], n, dyn, hT, range(KD), True, True)
                    ins.then_inc(tile_used, 1)
                    if t == 0 and first:
                        small_products()
                    if t == 0 and not first:
                        fox_pv(h - 2, 2)
                        fox_scores(h - 1, 3)
                    if t == 1 and not first:
                        fox_turn(h - 1)
                    if t == 2 and not first:
                        fox_pv(h - 1, 3)
                    if t == 6:
                        fox_scores(h, 0)
                    if t == 7:
                        fox_turn(h)
                    if t == 8:
                        pe.wait_ge(v_taken, i * TT + TT + FREE)
                        fox_pv(h, 0)
                        fox_scores(h + 1, 1)
                    if t == 9:
                        fox_turn(h + 1)
                    if t == 10:
                        fox_pv(h + 1, 1)
                        fox_scores(h + 2, 2)
                    if t == 11:
                        fox_turn(h + 2)

            fox(0, True)
            with pe.Fori(1, TURNS) as i:
                fox(i, False)
            fox_pv(FH - 2, 2)
            fox_scores(FH - 1, 3)
            fox_turn(FH - 1)
            fox_pv(FH - 1, 3)
            meet(pe, AFTER_FOX)

            def project(h, b, q, n, dyn, first):
                if q == 0:
                    if b >= 2:
                        pe.wait_ge(conv_read, h * 4 + (b - 1))
                    elif not first:
                        pe.wait_ge(z_read, h * 2 + (b - 1))
                ins = by_channel(pe, bank[b % 2][:, 0:T], n, dyn, hT, range(4 * q, 4 * q + 4), q == 0, q == 3)
                if q == 3:
                    ins.then_inc(tile_used, 1)

            def delta(j, pr, s, first):
                if s == 0:
                    pe.wait_ge(sq_ready, j + 1)
                    if not first:
                        pe.wait_ge(rhs_ready, j)
                    mm(bank[2][:, :], ones[:, :], sq[:, :, :].rearrange("p a b -> p (a b)"), start=True,
                       stop=True).then_inc(norms_summed, 1)
                if s == 1:
                    pe.wait_ge(SLg_ready, j * 6 + 6)
                    if not first:
                        pe.wait_ge(vn_ready, j * 2)
                        pe.wait_ge(X_ready, j * 26)
                    for ch in range(TT):
                        for v in range(2):
                            u = 2 * ch + v
                            ins = mm(bank[3][:, u * P:(u + 1) * P], SLg[:, v, ch, :], U[:, :], start=True, stop=True)
                    ins.then_inc(expo_made, 1)
                    for v in range(2):
                        ins = mm(bank[6][:, v * P:(v + 1) * P], gon[:, v, :], U[:, :], start=True, stop=True)
                    ins.then_inc(erow_made, 1)
                if s == 2:
                    pe.wait_ge(conv_done, j * 4 + 4)
                    if not first:
                        pe.wait_ge(ada2_biased, j)
                    for v in range(2):
                        for ch in range(TT):
                            at = (2 * v + ch) * P
                            ins = tr(bank[7][:, at:at + P], vc[:, pr, v, ch * P:(ch + 1) * P], ident[:, :])
                    ins.then_inc(v_turned, 1)
                if s == 3:
                    pe.wait_ge(qkn_ready, j * 2 + 2)
                    pe.wait_ge(norms_read, j + 1)
                    for ch in range(TT):
                        at = slice(ch * P, (ch + 1) * P)
                        ins = mm(bank[2][:, ch * T:(ch + 1) * T].rearrange("p (a b) -> p a b", a=2), qk[:, pr, 1, at],
                                 qk[:, pr, :, at], start=True, stop=True)
                    ins.then_inc(dots_made, 1)
                    if not first:
                        pe.wait_ge(osum_read, j)
                    tr(bank[5][:, 0:P], qk[:, pr, 1, 0:P], ident[:, :]).then_inc(k_turned, 1)
                if 5 <= s <= 16:
                    v, half = divmod(s - 5, 2)
                    for u in range(4):
                        if half == 0:
                            if v == 0 and u == 0:
                                pe.wait_ge(X_ready, j * 26 + 2)
                                pe.wait_ge(vtok_ready, j + 1)
                                pe.wait_ge(ktok_ready, j + 1)
                                pe.wait_ge(er_ready, j + 1)
                                if not first:
                                    pe.wait_ge(o_normed, j + FREE)
                            if u == 0:
                                pe.wait_ge(LTm_ready, j * 6 + (v + 1))
                            if v > 0:
                                pe.wait_ge(X_ready, j * 26 + (2 + 4 * (v - 1) + u + 1))
                            mm(bank[4 + u][:, 0:P], LTm[:, (v + 1) % 2, u, :], XX[:, u, 0, :], start=True,
                               stop=True).then_inc(Y_made, 1)
                        else:
                            pe.wait_ge(Y_ready, j * 24 + (4 * v + u + 1))
                            if 1 <= v < TRANSPOSED and u == 0:
                                pe.wait_ge(X_turned, j * (TRANSPOSED - 1) + v)
                            last = v + 1 == LEVELS - 1
                            if not last:
                                ins = mm(bank[4 + u][:, P:2 * P], XX[:, u, 1, :], Y[:, u, :], start=True, stop=True)
                            if v + 1 >= TRANSPOSED:
                                ins = mm(bank[4 + u][:, 2 * P:3 * P], Y[:, u, :], XX[:, u, 1, :], start=True, stop=True)
                            ins.then_inc(XY_made, 1)
                if s == 17:
                    pe.wait_ge(X_ready, j * 26 + 26)
                    pe.wait_ge(attn_ready, j * 2 + 2)
                    for v in range(2):
                        ins = mm(bank[2][:, v * P:(v + 1) * P], XX[:, v, 1, :], vtok[:, v, 0, :], start=True, stop=True)
                    ins.then_inc(u0_made, 1)
                if s == 18:
                    pe.wait_ge(u0_ready, j * 2 + 2)
                    pe.wait_ge(kd_ready, j * 2 + 2)
                    for v in range(2):
                        ins = mm(bank[3][:, v * P:(v + 1) * P], kd[:, v, :], u0[:, v, :], start=True, stop=True)
                    ins.then_inc(S_made, 1)
                if s == 19:
                    pe.wait_ge(S_ready, j + 1)
                    pe.wait_ge(qkg_ready, j * 2 + 2)
                    for v in range(2):
                        ins = mm(bank[2][:, T + v * P:T + (v + 1) * P], qkg[:, v, 1, :], S1[:, v, :], start=True, stop=True)
                    ins.then_inc(R_made, 1)
                if s == 20:
                    pe.wait_ge(rhs_ready, j + 1)
                    for v in range(2):
                        ins = mm(bank[3][:, T + v * P:T + (v + 1) * P], XX[:, 2 + v, 1, :], rhs1[:, v, :], start=True, stop=True)
                    ins.then_inc(vn_made, 1)
                if s == 21:
                    pe.wait_ge(vn_ready, j * 2 + 2)
                    for v in range(2):
                        o = bank[4]
                        mm(o[:, v * T:v * T + P], u0[:, v, :], attn[:, 0, v, :], start=True, stop=True)
                        mm(o[:, v * T + P:(v + 1) * T], S1[:, v, :], qkg[:, v, 0, :], start=True, stop=False)
                        ins = mm(o[:, v * T + P:(v + 1) * T], vn1[:, v, :], attn[:, 1, v, :], start=False, stop=True)
                    ins.then_inc(o_made, 1)
                if s == 22:
                    pe.wait_ge(osq_ready, j + 1)
                    mm(bank[5][:, :], ones[:, :], sq[:, :, :].rearrange("p a b -> p (a b)"), start=True,
                       stop=True).then_inc(osum_made, 1)
                if s == 23:
                    pe.wait_ge(ada2_used, j * (KD - 1) + (KD - 1))
                    for k in range(ADA_COLS // P):
                        ins = mm(bank[7][:, k:k + 1], acc2[:, k * P:(k + 1) * P], ones[:, 0:1], start=True, stop=True)
                    ins.then_inc(ada2_summed, 1)

            for b in range(DN_TILES):
                for q in range(4):
                    project(0, b, q, T_DN + b, 0, True)

            def gate_quarter(g, q):
                b, w = divmod(g, 2)
                if w == q == 0:
                    pe.wait_ge(z_read, 2 * (QKH - 1) + b + 1)
                ins = by_channel(pe, bank[b][:, w * T:(w + 1) * T], T_GATE + g, 0, hT, range(4 * q, 4 * q + 4),
                                 q == 0, q == 3)
                if q == 3:
                    ins.then_inc(tile_used, 1)

            def step(j, pr, n0, dyn, first=False, projecting=True):
                for s in range(SLOTS):
                    for q in (RUNS if projecting else GATE_RUNS)[s]:
                        if projecting:
                            project(j + 1, q // 4, q % 4, n0 + q // 4, dyn, False)
                        else:
                            gate_quarter(q // 4, q % 4)
                    delta(j, pr, s, first)

            step(0, 0, T_DN + DN_TILES, 0, first=True)
            with pe.Fori(0, QKH // 2 - 1) as i:
                step(i * 2 + 1, 1, T_DN + 2 * DN_TILES, i * (2 * DN_TILES))
                step(i * 2 + 2, 0, T_DN + 3 * DN_TILES, i * (2 * DN_TILES))
            step(QKH - 1, 1, 0, 0, projecting=False)
            meet(pe, AFTER_DN)

            def merge(i, blocks):
                n, dyn = T_MERGE, i * (4 * MERGE_TILES)
                oD_s, oF_s = (oD_hi, oD_lo), (oF_hi, oF_lo)
                for b in range(blocks):
                    y = bank[4 + 2 * (b % 2):6 + 2 * (b % 2)]
                    pe.wait_ge(merged, i * 4 + b + FREE - 1)
                    first = (o_lo, 0) if isinstance(i, int) and 4 * i + b == 0 else None
                    by_channel(pe, y[0][:, 0:T], n, dyn, oD_s, range(KD), True, False, 0, first).then_inc(tile_used, 1)
                    by_channel(pe, y[0][:, 0:T], n + 1, dyn, oD_s, range(KD), False, True, KD, first).then_inc(tile_used, 1)
                    by_channel(pe, y[1][:, 0:T], n + 2, dyn, oF_s, range(KD), True, True, 0,
                               first and (o_lo, 12)).then_inc(tile_used, 1)
                    n += 3
                    if not isinstance(i, int) or 4 * i + b < KD - 2:
                        pe.wait_ge(gates_ready, i * 4 + b + 1)
                        for w in range(2):
                            by_channel(pe, bank[b % 2][:, w * T:(w + 1) * T], n + w, dyn, hT, range(KD), True, True)\
                                .then_inc(tile_used, 1)
                        n += 2

            merge(0, 4)
            with pe.Fori(1, KD // 4 - 1) as i:
                merge(i, 4)
            merge(KD // 4 - 1, 4)
            meet(pe, AFTER_MERGE)

            def rows_of(n, grow):
                for g in range(4):
                    for k in range(4):
                        cols = gcol[:, n, 4 * g + k:4 * g + k + 1].broadcast_to([P, P])
                        ins = mm(bank[4 + g][:, k * P:(k + 1) * P], cols, ident[:, :], start=True, stop=True)
                ins.then_inc(grow, 1)

            rows_of(0, grow_made)
            with pe.Fori(0, D // GROUP // 2) as i:
                for t in range(2 * OUT_TILES):
                    g, k = divmod(t, OUT_TILES)
                    pe.wait_ge(m_lo, k + 1)
                    if k == 0:
                        pe.wait_ge(y_taken, i * (2 * TT) + (g * TT + TT))
                    by_token(pe, bank[2 * g:2 * g + 2], T_OUT + t, i * (2 * OUT_TILES), mT, 4 * k, 4, k == 0, k == OUT_TILES - 1)\
                        .then_inc(tile_used, 1)
            meet(pe, AFTER_OUT)
            pe.wait_ge(r_dve, 1 + 2 * TT)
            for g in range(8):
                for k in (2 * g, 2 * g + 1):
                    for t in range(TT):
                        at = (k % 2) * T + t * P
                        ins = mm(bank[g][:, at:at + P], x1[:, t, k * P:(k + 1) * P], diag[:, t, :], start=True, stop=True)
                ins.then_inc(h2_turned, 1)
            with pe.Fori(0, KF // 2) as i:
                for t in range(4):
                    b, w = divmod(t, 2)
                    if w == 0:
                        pe.wait_ge(gu_mixed, i * 2 + b + FREE - 1)
                    by_channel(pe, bank[2 * b + w][:, 0:T], T_FFN + t, i * 4, hT, range(KD), True, True, 0,
                               (h2_lo, 2) if t == 0 else None).then_inc(tile_used, 1)
            meet(pe, AFTER_FFN)
            rows_of(1, grow2_made)
            nd = len(DOWN_K)
            with pe.Fori(0, D // GROUP // 2) as i:
                for g in range(2):
                    for t, nk in enumerate(DOWN_K):
                        n = T_DOWN + g * nd + t
                        if t == 0:
                            pe.wait_ge(down_taken, i * (2 * TT) + (g * TT + TT))
                        by_token(pe, bank[2 * g:2 * g + 2], n, i * (2 * nd), guT, sum(DOWN_K[:t]), nk, t == 0, t == nd - 1)\
                            .then_inc(tile_used, 1)
            meet(pe, AFTER_DOWN)

        @block.vector
        def _(dve):
            V = nc.vector
            dve.wait_ge(made, 6)
            V.memset(brow[0:1, 1, VH:GATES], 0.0).then_inc(small_v, 1)
            def low_h(g):
                dve.wait_ge(h_hi, g + 1)
                V.tensor_tensor(hT[1][:, 4 * g:4 * g + 4, :], hf[:, 4 * g:4 * g + 4, :],
                                hT[0][:, 4 * g:4 * g + 4, :].bitcast(F32), ALU.subtract).then_inc(h_lo, 1)

            dve.wait_ge(cond_ready, 2)
            for a in range(2 * KD + 1):
                if a < 2 * KD:
                    add_ada(dve, a)
                if a == 5:
                    dve.wait_ge(x_squared, TT + 2)
                    for t in range(TT):
                        V.tensor_scalar(diag[:, t, :], ident[:, :], stat[:, 0, 1, t:t + 1], None, ALU.mult).then_inc(x_scaled, 1)
                if a % 4 == 0 and a > 0:
                    g = a // 4 - 1
                    at = slice(4 * (g // 2), 4 * (g // 2) + 4)
                    dve.wait_ge(ada_summed, g + 1)
                    V.tensor_tensor(adaT[:, g % 2, at], bank[5 + g % 2][:, 0:4],
                                    vecT[:, (g % 2) * KD + at.start:(g % 2) * KD + at.stop], ALU.add).then_inc(ada_biased, 1)
                    if g % 2 == 1:
                        dve.wait_ge(ada_biased, g + 1)
                        V.scalar_tensor_tensor(mod[:, 0, at], adaT[:, 1, at], 1.0, gain[0][:, at], ALU.add,
                                               ALU.mult).then_inc(mod_ready, 1)
                if a % 8 == 1 and a > 8:
                    low_h(a // 8 - 1)
            split_lo(dve, T_FOX)
            low_h(3)
            def log_decays():
                y, ny = small[:, 0, :, :], small[:, 4, :, :]
                dve.wait_ge(small_read, 2)
                V.tensor_tensor(small[:, 0, :, :], praw[:, :, VH:SMALL], bias_b[:, 0:1, :].broadcast_to([P, TT, GATES]),
                                ALU.add).then_inc(small_v, 1)
                dve.wait_ge(small_v, 2)
                V.tensor_scalar(small[:, 0, :, VH:GATES], small[:, 0, :, VH:GATES], -1.0, None, ALU.mult).then_inc(small_v, 1)
                dve.wait_ge(small_v, 3)
                V.tensor_scalar(ny, y, -1.0, None, ALU.mult).then_inc(small_v, 1)
                dve.wait_ge(small_v, 4)
                V.tensor_tensor(small[:, 1, :, :], y, ny, ALU.min).then_inc(small_v, 1)
                dve.wait_ge(small_v, 5)
                V.tensor_scalar(ny, y, 0.0, None, ALU.max).then_inc(small_v, 1)
                dve.wait_ge(small_v, 6)
                dve.wait_ge(small_s, 4)
                V.tensor_tensor(y, ny, small[:, 3, :, :], ALU.add).then_inc(small_v, 1)
                dve.wait_ge(small_v, 7)
                V.scalar_tensor_tensor(gd[:, :, 0:VH], y[:, :, 0:VH], -1.0, small[:, 5, 0:1, 0:VH].broadcast_to([P, TT, VH]),
                                       ALU.mult, ALU.mult).then_inc(decays_ready, 1)
                V.tensor_scalar(gd[:, :, VH:GATES], y[:, :, VH:GATES], -SQD, None, ALU.mult).then_inc(decays_ready, 1)
                dve.wait_ge(decays_ready, 2)

            dve.sem_inc(scores_masked, FREE)

            def fox_max(h):
                dve.wait_ge(scores_made, h + FREE + 1)
                dve.wait_ge(exp_made, h * 2 + FREE)
                V.tensor_tensor(fS[:, :, :], bank[4][:, 0:3 * P].rearrange("p (a b) -> p a b", a=3), CM[:, :, :],
                                ALU.add).then_inc(scores_masked, 1)
                dve.wait_ge(scores_masked, h + FREE + 1)
                V.tensor_reduce(fmax[:, 1:2], fS[:, 0:2, :].rearrange("p a b -> p (a b)"), AX.X, ALU.max).then_inc(max_made, 1)
                V.tensor_reduce(fmax[:, 0:1], fS[:, 2, :], AX.X, ALU.max).then_inc(max_made, 1)
                dve.wait_ge(max_made, h * 2 + 2)
                V.tensor_scalar(fneg[:, :], fmax[:, :], -SCALE, None, ALU.mult).then_inc(neg_made, 1)

            def fox_scale(h):
                dve.wait_ge(exp_made, h * 2 + 2 + FREE)
                V.reciprocal(finv[:, :], fsum[:, :]).then_inc(inv_made, 1)
                dve.wait_ge(inv_made, h + 1)
                V.tensor_scalar(fP[:, 0:2, :], fP[:, 0:2, :], finv[:, 1:2], None, ALU.mult).then_inc(probs_ready, 1)
                V.tensor_scalar(fP[:, 2, :], fP[:, 2, :], finv[:, 0:1], None, ALU.mult).then_inc(probs_ready, 1)

            def fox_turn(i, first):
                dyn, h = i * FOX_TILES, i * HEADS_A_TURN
                for t in range(FOX_TILES):
                    if t == (1 if first else 0):
                        if first:
                            log_decays()
                        dve.wait_ge(fL_ready, i * (3 * HEADS_A_TURN) + FREE)
                        V.tensor_copy(lfh[:, :, :], gd[:, :, bass.ds(i * HEADS_A_TURN + VH, HEADS_A_TURN)])\
                            .then_inc(lf_picked, 1)
                    head = {1: None if first else h - 1, 7: h, 9: h + 1, 11: h + 2}.get(t)
                    if head is not None:
                        fox_max(head)
                    split_lo(dve, T_FOX + t + 1, dyn)
                    if head is not None:
                        fox_scale(head)

            fox_turn(0, True)
            with dve.Fori(1, TURNS) as i:
                fox_turn(i, False)
            fox_max(FH - 1)
            fox_scale(FH - 1)
            meet(dve, AFTER_FOX)

            def conv_taps(h, b, pr):
                for tap in range(1, CONV_K):
                    if tap == 1:
                        dve.wait_ge(conv_first, h * 4 + (b + 1))
                    else:
                        dve.wait_ge(conv_added, h * 8 + (2 * b + tap - 1))
                    V.scalar_tensor_tensor(cacc[:, b % 2, tap:T], bank[b % 2][:, 0:T - tap],
                                           cw[:, pr, b, CONV_K - 1 - tap:CONV_K - tap], cacc[:, b % 2, tap:T],
                                           ALU.mult, ALU.add).then_inc(conv_read if tap == CONV_K - 1 else conv_added, 1)

            def pick_gates(h):
                V.tensor_copy(gh[:, :, :], gd[:, :, bass.ds(h * 2, 2)]).then_inc(gates_picked, 1)
                V.tensor_copy(bh[:, :, :], beta[:, :, bass.ds(h * 2, 2)]).then_inc(gates_picked, 1)

            def output(h):
                dve.wait_ge(orn_ready, h + 1)
                dve.wait_ge(oD_ready, h + FREE)
                V.scalar_tensor_tensor(on[:, :, :].rearrange("p a b -> p (a b)"), bank[4][:, :], nwcol,
                                       rno[:, :, :].rearrange("p a b -> p (a b)"), ALU.mult, ALU.mult).then_inc(o_normed, 1)

            def bias_ada2(j):
                dve.wait_ge(ada2_summed, j + 1)
                V.tensor_tensor(ada_flat[:, bass.ds(j * 4 + 2 * KD, 4)], bank[7][:, 0:4],
                                vecT[:, bass.ds(j * 4 + 2 * KD, 4)], ALU.add).then_inc(ada2_biased, 1)

            ada_flat = adaT[:, :, :].rearrange("p a k -> p (a k)")

            def step(j, pr, n0, dyn, first=False, project=True):
                for s in range(SLOTS):
                    for q in (RUNS if project else GATE_RUNS)[s]:
                        split_lo(dve, n0 + q // 4 + 1, dyn, TILE, ((q % 4, q % 4 + 1),))
                    if s == 0:
                        if not first:
                            dve.wait_ge(vn_ready, j * 2)
                            dve.wait_ge(SLg_ready, j * 6)
                        pick_gates(j)
                    if s == 1:
                        if not first:
                            bias_ada2(j - 1)
                        dve.wait_ge(rn_ready, j + 1)
                        V.scalar_tensor_tensor(qk[:, pr, 0, :], qk[:, pr, 0, :], SCALE, rn[:, 0, :], ALU.mult,
                                               ALU.mult).then_inc(qkn_ready, 1)
                        V.tensor_tensor(qk[:, pr, 1, :], qk[:, pr, 1, :], rn[:, 1, :], ALU.mult).then_inc(qkn_ready, 1)
                    if s == 2 and not first:
                        output(j - 1)
                    if s == 3:
                        dve.wait_ge(dots_made, j + 1)
                        dve.wait_ge(E_ready, j + 1)
                        dve.wait_ge(gates_picked, j * 2 + 2)
                        if not first:
                            dve.wait_ge(LTm_ready, j * 6)
                        for u in range(4):
                            ch, v = divmod(u, 2)
                            V.scalar_tensor_tensor(LT[:, u, :], bank[2][:, ch * T + P:(ch + 1) * T], bh[:, ch, v:v + 1],
                                                   E[:, ch, v, :], ALU.mult, ALU.mult).then_inc(LT_ready, 1)
                        dve.wait_ge(LT_ready, j * 4 + 4)
                        if not first:
                            dve.wait_ge(vn_made, j)
                        V.tensor_tensor(Y[:, :, :], LT[:, :, :], LM[:, 0:1, :].broadcast_to([P, 4, P]),
                                        ALU.mult).then_inc(L1_ready, 1)
                        dve.wait_ge(L1_ready, j + 1)
                        V.tensor_tensor(XX[:, :, 1, :], ident[:, :].unsqueeze(1).broadcast_to([P, 4, P]), Y[:, :, :],
                                        ALU.subtract).then_inc(X_ready, 1)
                        dve.wait_ge(X_ready, j * 26 + 1)
                        V.transpose(XX[:, :, 0, :], XX[:, :, 1, :]).then_inc(X_ready, 1)
                    if s in (6, 8, 10, 12, 14, 16):
                        v = (s - 6) // 2
                        for u in range(4):
                            dve.wait_ge(XY_made, j * 24 + (4 * v + u + 1))
                            if v + 1 < TRANSPOSED:
                                V.tensor_tensor(XX[:, u, 0, :], XX[:, u, 0, :], bank[4 + u][:, P:2 * P],
                                                ALU.subtract).then_inc(X_ready, 1)
                                continue
                            if v < LEVELS - 2:
                                at, src = XX[:, u, :, :].rearrange("p a b -> p (a b)"), bank[4 + u][:, P:3 * P]
                            else:
                                at, src = XX[:, u, 1, :], bank[4 + u][:, 2 * P:3 * P]
                            V.tensor_tensor(at, at, src, ALU.subtract).then_inc(X_ready, 1)
                        if v + 1 < TRANSPOSED:
                            dve.wait_ge(X_ready, j * 26 + (2 + 4 * v + 4))
                            V.transpose(XX[:, :, 1, :], XX[:, :, 0, :]).then_inc(X_turned, 1)
                    if s == 19:
                        dve.wait_ge(R_made, j + 1)
                        V.tensor_tensor(rhs1[:, :, :], vtok[:, :, 1, :], bank[2][:, T:2 * T].rearrange("p (a b) -> p a b", a=2),
                                        ALU.subtract).then_inc(rhs_ready, 1)
                    for b in range(4):
                        if project and s == CONV_SLOTS[b]:
                            conv_taps(j + 1, b, 1 - pr)
                    if s in (9, 13):
                        ch = (s - 9) // 4
                        dve.wait_ge(Em_ready, j + 1)
                        if not first:
                            dve.wait_ge(o_made, j)
                        V.tensor_tensor(attn[:, ch, :, :], bank[2][:, ch * T:ch * T + P].unsqueeze(1).broadcast_to([P, 2, P]),
                                        Em[:, ch, :, :], ALU.mult).then_inc(attn_ready, 1)
                if not project:
                    output(j)
                    bias_ada2(j)

            for b in range(DN_TILES):
                split_lo(dve, T_DN + b + 1)
                if 1 <= b <= 4:
                    conv_taps(0, b - 1, 0)
            step(0, 0, T_DN + DN_TILES, 0, first=True)
            with dve.Fori(0, QKH // 2 - 1) as i:
                step(i * 2 + 1, 1, T_DN + 2 * DN_TILES, i * (2 * DN_TILES))
                step(i * 2 + 2, 0, T_DN + 3 * DN_TILES, i * (2 * DN_TILES))
            step(QKH - 1, 1, T_GATE, 0, project=False)
            meet(dve, AFTER_DN)

            dve.sem_inc(merged, FREE)
            V.scalar_tensor_tensor(mod[:, 1, :], adaT[:, 4, :], 1.0, gain[2], ALU.add, ALU.mult).then_inc(mod2_ready, 1)
            V.tensor_tensor(gcol[:, 0, :], adaT[:, 2, :], gain[1], ALU.mult).then_inc(mod2_ready, 1)
            V.tensor_tensor(gcol[:, 1, :], adaT[:, 5, :], gain[3], ALU.mult).then_inc(mod2_ready, 1)
            def low_outputs(part):
                for g in range(4 * part, 4 * part + 4):
                    src, lo, hi, k = (oD, oD_lo, oD_hi, 4 * g) if g < 8 else (oF, oF_lo, oF_hi, 4 * (g - 8))
                    dve.wait_ge(o_hi, g + 1)
                    V.tensor_tensor(lo[:, k:k + 4, :], src[:, k:k + 4, :], hi[:, k:k + 4, :].bitcast(F32),
                                    ALU.subtract).then_inc(o_lo, 1)

            def merge(i, blocks):
                n, dyn = T_MERGE, i * (4 * MERGE_TILES)
                for b in range(blocks):
                    blk = i * 4 + b
                    tiles = MERGE_TILES if not isinstance(i, int) or blk < KD - 2 else 3
                    for t in range(tiles):
                        if isinstance(i, int) and 4 * i + b == 0 and t < 3:
                            low_outputs(t)
                        split_lo(dve, n + t + 1, dyn)
                        if t == 2:
                            used(dve, n + 2, dyn)
                            dve.wait_ge(gates_ready, blk + 1)
                            for w in range(2):
                                V.tensor_tensor(mt[:, w, :], gt[:, b % 2, w * T:(w + 1) * T],
                                                bank[4 + 2 * (b % 2) + w][:, 0:T], ALU.mult).then_inc(part_made, 1)
                            dve.wait_ge(part_made, blk * 2 + 2)
                            V.tensor_tensor(mF[:, bass.ds(blk, 1), :], mt[:, 0:1, :], mt[:, 1:2, :], ALU.add).then_inc(merged, 1)
                    n += tiles

            merge(0, 4)
            with dve.Fori(1, KD // 4 - 1) as i:
                merge(i, 4)
            merge(KD // 4 - 1, 4)
            meet(dve, AFTER_MERGE)
            for g in range(4):
                dve.wait_ge(m_hi, g + 1)
                V.tensor_tensor(mT[1][:, 4 * g:4 * g + 4, :], mF[:, 4 * g:4 * g + 4, :],
                                mT[0][:, 4 * g:4 * g + 4, :].bitcast(F32), ALU.subtract).then_inc(m_lo, 1)
            def gate_group(y, grow, g, squared, taken):
                at = slice(g * GROUP, (g + 1) * GROUP)
                dve.wait_ge(squared, (g + 1) * TT)
                for t in range(TT):
                    V.tensor_tensor(y[:, t, at], bank[2 * (g % 2) + t][:, :], grow[:, at], ALU.mult).then_inc(taken, 1)

            dve.sem_inc(y_taken, 2 * TT)
            dve.wait_ge(grow_taken, 4)
            for t in range(GROUPS * OUT_TILES):
                split_lo(dve, T_OUT + t + 1)
                if t % OUT_TILES == 0 and t:
                    gate_group(ysb, Grow, t // OUT_TILES - 1, y_squared, y_taken)
            gate_group(ysb, Grow, GROUPS - 1, y_squared, y_taken)
            meet(dve, AFTER_OUT)
            V.tensor_reduce(stat[:, 1, 0, :], part[:, 0, :, :], AX.X, ALU.add).then_inc(r_dve, 1)
            dve.wait_ge(x1_landed, 16)
            dve.wait_ge(r_act, 2)
            for t in range(TT):
                V.scalar_tensor_tensor(x1[:, t, :], ysb[:, t, :], stat[:, 1, 1, t:t + 1], x1[:, t, :], ALU.mult,
                                       ALU.add).then_inc(r_dve, 1)
            split_lo(dve, T_FFN + 1)
            dve.wait_ge(r_act, 4 + TT)
            for t in range(TT):
                V.tensor_scalar(diag[:, t, :], ident[:, :], stat[:, 2, 1, t:t + 1], None, ALU.mult).then_inc(r_dve, 1)
            def low_h2(m):
                dve.wait_ge(h2_hi, m + 1)
                V.tensor_tensor(hT[1][:, 4 * m:4 * m + 4, :], h2f[:, 4 * m:4 * m + 4, :],
                                hT[0][:, 4 * m:4 * m + 4, :].bitcast(F32), ALU.subtract).then_inc(h2_lo, 1)

            for m in range(4):
                g = 2 * m
                dve.wait_ge(h2_turned, g + 1)
                for k in (2 * g, 2 * g + 1):
                    V.tensor_scalar(h2f[:, k, :], bank[g][:, (k % 2) * T:(k % 2 + 1) * T], mod[:, 1, k:k + 1],
                                    adaT[:, 3, k:k + 1], ALU.mult, ALU.add).then_inc(h2_mod_dve, 1)
                if m > 0:
                    low_h2(m - 1)
            low_h2(3)
            dve.wait_ge(h2_lo, 4)
            dve.sem_inc(gu_mixed, FREE)
            def ffn(i):
                for t in range(4):
                    b, w = divmod(t, 2)
                    if t or not isinstance(i, int):
                        split_lo(dve, T_FFN + t + 1, i * 4)
                    if w == 1:
                        used(dve, T_FFN + t, i * 4)
                        dve.wait_ge(silu_made, i * 2 + (b + 1))
                        V.tensor_tensor(guf[:, b, :], sg[:, b, :], bank[2 * b + 1][:, 0:T], ALU.mult).then_inc(gu_mixed, 1)
                        dve.wait_ge(gu_hi, i * 2 + (b + 1))
                        V.tensor_tensor(guT[1][:, bass.ds(i * 2 + b, 1), :], guf[:, b:b + 1, :],
                                        guT[0][:, bass.ds(i * 2 + b, 1), :].bitcast(F32), ALU.subtract).then_inc(gu_lo, 1)

            ffn(0)
            with dve.Fori(1, KF // 2) as i:
                ffn(i)
            meet(dve, AFTER_FFN)
            dve.sem_inc(down_taken, 2 * TT)
            dve.wait_ge(grow2_taken, 4)
            nd = len(DOWN_K)
            for t in range(GROUPS * nd):
                if t < GROUPS * nd - 1:
                    split_lo(dve, T_DOWN + t + 1, 0, DOWN_K[(t + 1) % nd] * GROUP)
                if t % nd == 0 and t:
                    gate_group(y2, Grow2, t // nd - 1, down_squared, down_taken)
            gate_group(y2, Grow2, GROUPS - 1, down_squared, down_taken)
            meet(dve, AFTER_DOWN)
            V.tensor_reduce(stat[:, 3, 0, :], part[:, 1, :, :], AX.X, ALU.add).then_inc(f_dve, 1)
            dve.wait_ge(f_act, 2)
            for t in range(TT):
                for half in range(2):
                    at = slice(half * D // 2, (half + 1) * D // 2)
                    V.scalar_tensor_tensor(x1[:, t, at], y2[:, t, at], stat[:, 3, 1, t:t + 1], x1[:, t, at], ALU.mult,
                                           ALU.add).then_inc(f_dve, 1)


_INS = ["x", "c", "w_ada", "b_ada", "norm_gains", "w_in", "dn_conv", "dn_a_log", "dn_dt_bias", "dn_norm_w",
        "fox_f_bias", "w_branch_dn", "w_branch_fox", "w_out", "w_gate", "w_up", "w_down"]
_OUT = ((1, T, D), "float32")


def kernel(**inputs):
    import numpy as _np
    import concourse.bacc as _bacc
    from concourse import mybir as _mybir
    from concourse.bass_utils import run_bass_kernel_spmd as _run

    nc = _bacc.Bacc("TRN2", target_bir_lowering=False, num_devices=1, dynamic_dma_scratch_size=1024)
    arrays, args = {}, []
    for name in _INS:
        a = _np.ascontiguousarray(inputs[name])
        arrays[f"in_{name}_dram"] = a
        args.append(nc.dram_tensor(f"in_{name}_dram", a.shape, _mybir.dt.from_np(a.dtype), kind="ExternalInput").ap())
    shape, dtype = _OUT
    args.append(nc.dram_tensor("out_0_dram", shape, _mybir.dt.from_np(_np.dtype(dtype)), kind="ExternalOutput").ap())
    build(nc, *args)
    r = _run(nc, [arrays], core_ids=[0])
    return r.results[0]["out_0_dram"]
```
